# Optimizing a Trainium2 kernel written in Bass

```python
import math
import jax, jax.numpy as jnp
from jax import lax
import numpy as np

D_MODEL = 1024
BATCH = 1
SEQ = 2048
DEPTH = 1

N_MIXERS = 4
BLOCK = 128
EPS = 1e-6
SB_HEADS = 16
SB_HEAD_DIM = D_MODEL // SB_HEADS
SB_WIDTH = SB_HEADS * SB_HEAD_DIM
GM_WIDTH = 2 * D_MODEL
GM_CHUNK = 128
GM_GROUPS = 16
CV_WIDTH = 2 * D_MODEL
CV_KERNEL = 31
FX_HEADS = 16
FX_HEAD_DIM = D_MODEL // FX_HEADS
FX_WIDTH = FX_HEADS * FX_HEAD_DIM

kernel_name = "hybrid_sb_gmlp_conv_fox_trunk"

def _layer_counts():
    return [len(range(kind, DEPTH, N_MIXERS)) for kind in range(N_MIXERS)]

def rmsnorm(x, g):
    xf = x.astype(jnp.float32)
    y = xf * lax.rsqrt(jnp.mean(xf * xf, axis=-1, keepdims=True) + EPS)
    return (y * g.astype(jnp.float32)).astype(x.dtype)

def layernorm(x, g, b):
    xf = x.astype(jnp.float32)
    mu = jnp.mean(xf, axis=-1, keepdims=True)
    xc = xf - mu
    var = jnp.mean(xc * xc, axis=-1, keepdims=True)
    y = xc * lax.rsqrt(var + EPS) * g.astype(jnp.float32) + b.astype(jnp.float32)
    return y.astype(x.dtype)

def stick_breaking_attention(q, k, v):
    B, S, H, Dh = q.shape
    scale = 1.0 / math.sqrt(Dh)
    outs = []
    for t0 in range(0, S, BLOCK):
        kend = t0 + BLOCK
        z = jnp.einsum('bthd,bshd->bhts', q[:, t0:kend], k[:, :kend]).astype(jnp.float32) * scale
        t_idx = t0 + jnp.arange(BLOCK)[:, None]
        s_idx = jnp.arange(kend)[None, :]
        mask = s_idx < t_idx
        log_beta = jax.nn.log_sigmoid(z)
        log_rem = jnp.where(mask, jax.nn.log_sigmoid(-z), 0.0)
        after = lax.cumsum(log_rem, axis=3, reverse=True) - log_rem
        w = jnp.where(mask, jnp.exp(log_beta + after), 0.0)
        outs.append(jnp.einsum('bhts,bshd->bthd', w.astype(v.dtype), v[:, :kend]))
    return jnp.concatenate(outs, axis=1)

def forgetting_attention(q, k, v, log_f):
    B, S, H, Dh = q.shape
    scale = 1.0 / math.sqrt(Dh)
    cum = jnp.cumsum(log_f, axis=1).transpose(0, 2, 1)
    outs = []
    for t0 in range(0, S, BLOCK):
        kend = t0 + BLOCK
        logits = jnp.einsum('bthd,bshd->bhts', q[:, t0:kend], k[:, :kend]).astype(jnp.float32) * scale
        logits = logits + cum[:, :, t0:kend, None] - cum[:, :, None, :kend]
        t_idx = t0 + jnp.arange(BLOCK)[:, None]
        s_idx = jnp.arange(kend)[None, :]
        p = jax.nn.softmax(jnp.where(s_idx <= t_idx, logits, -jnp.inf), axis=-1)
        outs.append(jnp.einsum('bhts,bshd->bthd', p.astype(v.dtype), v[:, :kend]))
    return jnp.concatenate(outs, axis=1)

def mixer_stick_breaking(h, w_in, w_out):
    B, S, _ = h.shape
    proj = jnp.einsum('bsd,de->bse', h, w_in)
    q, k, v, g = jnp.split(proj, 4, axis=-1)
    hs = (B, S, SB_HEADS, SB_HEAD_DIM)
    o = stick_breaking_attention(q.reshape(hs), k.reshape(hs), v.reshape(hs)).reshape(B, S, SB_WIDTH)
    return jnp.einsum('bse,ed->bsd', o * jax.nn.silu(g), w_out)

def mixer_chunked_gmlp(h, w_in, v_ln_g, v_ln_b, w_s, b_s, w_out):
    B, S, _ = h.shape
    proj = jnp.einsum('bsd,de->bse', h, w_in)
    uv, g = proj[..., :2 * GM_WIDTH], proj[..., 2 * GM_WIDTH:]
    uv = jax.nn.gelu(uv)
    u, v = jnp.split(uv, 2, axis=-1)
    v = layernorm(v, v_ln_g, v_ln_b)
    tril = jnp.tril(jnp.ones((GM_CHUNK, GM_CHUNK), w_s.dtype))
    vc = v.reshape(B, S // GM_CHUNK, GM_CHUNK, GM_GROUPS, GM_WIDTH // GM_GROUPS)
    s = jnp.einsum('gts,bnsgc->bntgc', w_s * tril, vc) + b_s.T[None, None, :, :, None]
    o = u * s.reshape(B, S, GM_WIDTH)
    return jnp.einsum('bse,ed->bsd', o * jax.nn.silu(g), w_out)

def mixer_conformer_conv(h, w_in, conv_w, conv_b, ln_g, ln_b, w_out):
    proj = jnp.einsum('bsd,de->bse', h, w_in)
    a, b, g = jnp.split(proj, 3, axis=-1)
    y = a * jax.nn.sigmoid(b)
    y = lax.conv_general_dilated(
        y, conv_w[:, None, :], window_strides=(1,), padding=[(CV_KERNEL - 1, 0)],
        dimension_numbers=('NWC', 'WIO', 'NWC'), feature_group_count=CV_WIDTH) + conv_b
    y = jax.nn.silu(layernorm(y, ln_g, ln_b))
    return jnp.einsum('bse,ed->bsd', y * jax.nn.silu(g), w_out)

def mixer_forgetting(h, w_in, b_f, w_out):
    B, S, _ = h.shape
    proj = jnp.einsum('bsd,de->bse', h, w_in)
    q = proj[..., :FX_WIDTH]
    k = proj[..., FX_WIDTH:2 * FX_WIDTH]
    v = proj[..., 2 * FX_WIDTH:3 * FX_WIDTH]
    g = proj[..., 3 * FX_WIDTH:4 * FX_WIDTH]
    f_logit = proj[..., 4 * FX_WIDTH:].astype(jnp.float32) + b_f.astype(jnp.float32)
    log_f = jax.nn.log_sigmoid(f_logit)
    hs = (B, S, FX_HEADS, FX_HEAD_DIM)
    o = forgetting_attention(q.reshape(hs), k.reshape(hs), v.reshape(hs), log_f).reshape(B, S, FX_WIDTH)
    return jnp.einsum('bse,ed->bsd', o * jax.nn.silu(g), w_out)

def setup_inputs(seed: int = 0) -> dict:
    key = jax.random.key(seed)
    ks = iter(jax.random.split(key, 32))
    nA, nB, nC, nD = _layer_counts()
    f32 = jnp.float32

    def nrm(shape, scale):
        return jax.random.normal(next(ks), shape, f32) * scale

    def gain(n, width):
        return 1.0 + nrm((n, width), 0.02)

    d_in = D_MODEL ** -0.5
    return {
        "x": nrm((BATCH, SEQ, D_MODEL), 1.0),
        "a_norm": gain(nA, D_MODEL),
        "a_w_in": nrm((nA, D_MODEL, 4 * SB_WIDTH), d_in),
        "a_w_out": nrm((nA, SB_WIDTH, D_MODEL), SB_WIDTH ** -0.5),
        "b_norm": gain(nB, D_MODEL),
        "b_w_in": nrm((nB, D_MODEL, 3 * GM_WIDTH), d_in),
        "b_v_ln_g": gain(nB, GM_WIDTH),
        "b_v_ln_b": nrm((nB, GM_WIDTH), 0.02),
        "b_w_s": nrm((nB, GM_GROUPS, GM_CHUNK, GM_CHUNK), GM_CHUNK ** -0.5),
        "b_b_s": 1.0 + nrm((nB, GM_GROUPS, GM_CHUNK), 0.1),
        "b_w_out": nrm((nB, GM_WIDTH, D_MODEL), GM_WIDTH ** -0.5),
        "c_norm": gain(nC, D_MODEL),
        "c_w_in": nrm((nC, D_MODEL, 3 * CV_WIDTH), d_in),
        "c_conv_w": nrm((nC, CV_KERNEL, CV_WIDTH), CV_KERNEL ** -0.5),
        "c_conv_b": nrm((nC, CV_WIDTH), 0.02),
        "c_ln_g": gain(nC, CV_WIDTH),
        "c_ln_b": nrm((nC, CV_WIDTH), 0.02),
        "c_w_out": nrm((nC, CV_WIDTH, D_MODEL), CV_WIDTH ** -0.5),
        "d_norm": gain(nD, D_MODEL),
        "d_w_in": nrm((nD, D_MODEL, 4 * FX_WIDTH + FX_HEADS), d_in),
        "d_b_f": 3.0 + nrm((nD, FX_HEADS), 0.5),
        "d_w_out": nrm((nD, FX_WIDTH, D_MODEL), FX_WIDTH ** -0.5),
        "final_norm": 1.0 + nrm((D_MODEL,), 0.02),
    }

def reference(x, a_norm, a_w_in, a_w_out, b_norm, b_w_in, b_v_ln_g, b_v_ln_b, b_w_s, b_b_s, b_w_out,
              c_norm, c_w_in, c_conv_w, c_conv_b, c_ln_g, c_ln_b, c_w_out,
              d_norm, d_w_in, d_b_f, d_w_out, final_norm):
    for i in range(DEPTH):
        kind, j = i % N_MIXERS, i // N_MIXERS
        if kind == 0:
            x = x + mixer_stick_breaking(rmsnorm(x, a_norm[j]), a_w_in[j], a_w_out[j])
        elif kind == 1:
            x = x + mixer_chunked_gmlp(rmsnorm(x, b_norm[j]), b_w_in[j], b_v_ln_g[j], b_v_ln_b[j],
                                       b_w_s[j], b_b_s[j], b_w_out[j])
        elif kind == 2:
            x = x + mixer_conformer_conv(rmsnorm(x, c_norm[j]), c_w_in[j], c_conv_w[j], c_conv_b[j],
                                         c_ln_g[j], c_ln_b[j], c_w_out[j])
        else:
            x = x + mixer_forgetting(rmsnorm(x, d_norm[j]), d_w_in[j], d_b_f[j], d_w_out[j])
    return rmsnorm(x, final_norm)


_drawn_inputs = setup_inputs


def setup_inputs(seed=0):
    import zlib

    import numpy as np

    out = dict(_drawn_inputs(seed))
    spreads = {}
    factors = {'a_norm': 4.658, 'final_norm': 2.825}
    for name, (base, spread) in spreads.items():
        noise = np.random.default_rng([zlib.crc32(name.encode()), seed]).standard_normal(out[name].shape)
        drawn = base * np.exp(spread * noise) if base else spread * noise
        out[name] = __import__('jax').numpy.asarray(drawn.astype(out[name].dtype))
    for name, factor in factors.items():
        out[name] = (out[name] * factor).astype(out[name].dtype)
    return out
```

```python
import concourse.bass as bass
from concourse import mybir
from contextlib import ExitStack

F32 = mybir.dt.float32
F32R = mybir.dt.float32r
BF16 = mybir.dt.bfloat16
ALU = mybir.AluOpType
ACT = mybir.ActivationFunctionType

P = 128
S = 2048
D = 1024
H = 16
DH = D // H
KT = D // P
NB = S // P
CH = 512
NC = S // CH
CB = CH // P
EPS = 1e-6
Z_SCALE = DH ** -0.5
MASKED = -1e30


def as_f32(ap):
    return ap.bitcast(F32)


def pass_waits(eng, passed):
    eng.sem_inc(passed, 1)


def rms_chain(nc, dve, chain, count, mean_sq, root, recip, tmp):
    def link(ins):
        nonlocal count
        ins.then_inc(chain, 1)
        count = count + 1
        dve.wait_ge(chain, count)
    link(nc.vector.reciprocal(recip, root))
    link(nc.vector.tensor_tensor(tmp, recip, recip, ALU.mult))
    link(nc.vector.tensor_tensor(tmp, tmp, mean_sq, ALU.mult))
    link(nc.vector.tensor_scalar(tmp, tmp, -0.5, 1.5, ALU.mult, ALU.add))
    link(nc.vector.tensor_tensor(recip, recip, tmp, ALU.mult))
    return count


CHAIN = 5


def phase_norm_and_v(nc, x, a_norm, w_v, v_dram, hT_hi, hT_lo, ident):
    with ExitStack() as ctx:
        def sb(name, shape, dt):
            return ctx.enter_context(nc.sbuf_tensor(name, shape, dt))

        def pb(name):
            return ctx.enter_context(nc.psum_tensor(name, [P, CH], F32))

        def sem(name):
            return ctx.enter_context(nc.semaphore(name))

        w_raw = sb("wv_raw", [P, 2, 2, CH], F32)
        w_hi = sb("wv_hi", [P, KT, CH], F32R)
        w_lo = sb("wv_lo", [P, KT, CH], F32R)
        xt = sb("xt", [P, 2, D], F32)
        norm_row = sb("a_norm_row", [P, D], F32)
        junk = sb("square_junk", [P, D], BF16)
        stg_hi = [sb(f"stage_hi{p}", [P, KT, P], F32R) for p in range(2)]
        stg_lo = [sb(f"stage_lo{p}", [P, KT, P], F32R) for p in range(2)]
        vst = sb("v_stage", [P, 2, CH], F32)
        stat = sb("stat", [P, 2, 5], F32)
        zeros = sb("zeros", [D // CH, CH], F32)
        tp = [[pb(f"hT_ps{p}{q}") for q in range(2)] for p in range(2)]
        vp = [pb(f"v_ps{p}") for p in range(2)]

        s_ident = sem("ident_ready")
        s_norm = sem("norm_row_loaded")
        s_x = [sem(f"x_loaded{p}") for p in range(2)]
        s_wraw = [sem(f"wv_raw_loaded{p}") for p in range(2)]
        s_whi = sem("wv_hi_ready")
        s_wlo = sem("wv_lo_ready")
        s_sumsq = sem("sum_squares_ready")
        s_mean = sem("mean_square_ready")
        s_root = sem("root_ready")
        s_chain = sem("rms_chain")
        s_h = sem("h_ready")
        s_tr = sem("h_transposed")
        s_hi = sem("stage_hi_ready")
        s_lo = sem("stage_lo_ready")
        s_keep_hi = sem("hT_hi_kept")
        s_keep_lo = sem("hT_lo_kept")
        s_v = sem("v_ready")
        s_vst = sem("v_evacuated")
        s_vout = [sem(f"v_stored{p}") for p in range(2)]
        s_stage = sem("stage_reloaded")
        s_passed = sem("waits_passed_norm")
        s_zero = sem("zero_row")
        s_zout = sem("zero_row_stored")

        NPASS = 2
        QW = KT // 2

        with nc.Block() as block:
            @block.sync
            def _(sp):
                sp.dma_start(norm_row[:], a_norm.rearrange("(a n) -> a n", a=1).to_broadcast([P, D])).then_inc(s_norm, 16)
                for p in range(2):
                    sp.dma_start(xt[:, p, :], x[p * P:(p + 1) * P, :]).then_inc(s_x[p], 16)

                def load_w(n):
                    half, q = n // QW, n % QW
                    if n >= 2:
                        sp.wait_ge(s_wlo, n - 1)
                    sp.dma_start(w_raw[:, n % 2, :, :],
                                 w_v[half, :, 2 * q:2 * q + 2, :]).then_inc(s_wraw[n % 2], 16)
                for n in range(QW):
                    load_w(n)
                with sp.Fori(1, NB // 2) as i:
                    for p in range(2):
                        sp.wait_ge(s_tr, 2 * i + p - 1)
                        sp.dma_start(xt[:, p, :], x[bass.ts(2 * i + p, P), :]).then_inc(s_x[p], 16)
                for n in range(QW, 2 * QW):
                    load_w(n)
                sp.wait_ge(s_zero, 1)
                sp.dma_start(v_dram[S, :].rearrange("(a n) -> a n", n=CH), zeros[:]).then_inc(s_zout, 16)
                sp.wait_ge(s_zout, 16)
                for p in range(2):
                    sp.wait_ge(s_vout[p], 16 * NB)

            @block.gpsimd
            def _(pool):
                nc.gpsimd.memset(ident[:], 0.0).then_inc(s_ident, 1)
                pool.wait_ge(s_ident, 1)
                nc.gpsimd.affine_select(out=ident[:], in_=ident[:], compare_op=ALU.not_equal, fill=1.0, base=0,
                                        pattern=[[-1, P]], channel_multiplier=1).then_inc(s_ident, 1)

                def split_w(n):
                    q = n % QW
                    pool.wait_ge(s_wraw[n % 2], 16 * (n // 2 + 1))
                    pool.wait_ge(s_whi, n + 1)
                    nc.gpsimd.tensor_tensor(w_lo[:, 2 * q:2 * q + 2, :], w_raw[:, n % 2, :, :],
                                            as_f32(w_hi[:, 2 * q:2 * q + 2, :]), ALU.subtract).then_inc(s_wlo, 1)
                for n in range(QW):
                    split_w(n)
                with pool.Fori(0, NB // 2) as i:
                    for p in range(2):
                        pool.wait_ge(s_lo, 4 * i + 2 * p + 2)
                        pass_waits(pool, s_passed)
                        nc.gpsimd.tensor_copy(hT_lo[:, :, bass.ts(2 * i + p, P)], as_f32(stg_lo[p][:])).then_inc(s_keep_lo, 1)
                pool.wait_ge(s_v, NB)
                for n in range(QW, 2 * QW):
                    split_w(n)

            @block.scalar
            def _(act):
                def squares(s, p, first=False):
                    act.wait_ge(s_x[p], 8 * (s - p) + 16)
                    if not first:
                        act.wait_ge(s_sumsq, s)
                    nc.scalar.activation(junk[:], xt[:, p, :], ACT.Square,
                                         accum_out=stat[:, p, 0:1]).then_inc(s_sumsq, 1)

                def root(s, p):
                    act.wait_ge(s_mean, s + 1)
                    nc.scalar.activation(stat[:, p, 2:3], stat[:, p, 1:2], ACT.Sqrt).then_inc(s_root, 1)

                def stage_hi(s, p, first):
                    act.wait_ge(s_tr, s + 1)
                    if not first:
                        act.wait_ge(s_v, s - 1)
                        act.wait_ge(s_keep_hi, s - 1)
                    for q in range(2):
                        nc.scalar.activation(stg_hi[p][:, 4 * q:4 * q + 4, :].rearrange("p k t -> p (k t)"),
                                             tp[p][q][:], ACT.Copy).then_inc(s_hi, 1)

                def evacuate(s, p, first):
                    act.wait_ge(s_v, s + 1)
                    if not first:
                        act.wait_ge(s_vout[p], 8 * (s - p))
                    nc.scalar.activation(vst[:, p, :], vp[p][:], ACT.Copy).then_inc(s_vst, 1)

                def store(s, p, rows, half):
                    act.wait_ge(s_vst, s + 1)
                    act.dma_start(v_dram[rows, half * CH:(half + 1) * CH], vst[:, p, :]).then_inc(s_vout[p], 16)

                def hi_w(n):
                    q = n % QW
                    act.wait_ge(s_wraw[n % 2], 16 * (n // 2 + 1))
                    nc.scalar.activation(w_hi[:, 2 * q:2 * q + 2, :], w_raw[:, n % 2, :, :], ACT.Copy).then_inc(s_whi, 1)

                squares(0, 0, True)
                root(0, 0)
                for n in range(QW):
                    hi_w(n)
                squares(1, 1)
                root(1, 1)
                stage_hi(0, 0, True)
                squares(2, 0)
                root(2, 0)
                stage_hi(1, 1, True)
                evacuate(0, 0, True)
                store(0, 0, slice(0, P), 0)
                squares(3, 1)
                root(3, 1)
                stage_hi(2, 0, False)
                evacuate(1, 1, True)
                store(1, 1, slice(P, 2 * P), 0)
                with act.Fori(1, NB // 2 - 1) as i:
                    squares(2 * i + 2, 0)
                    root(2 * i + 2, 0)
                    stage_hi(2 * i + 1, 1, False)
                    evacuate(2 * i, 0, False)
                    store(2 * i, 0, bass.ts(2 * i, P), 0)
                    squares(2 * i + 3, 1)
                    root(2 * i + 3, 1)
                    stage_hi(2 * i + 2, 0, False)
                    evacuate(2 * i + 1, 1, False)
                    store(2 * i + 1, 1, bass.ts(2 * i + 1, P), 0)
                stage_hi(NB - 1, 1, False)
                for s in (NB - 2, NB - 1):
                    evacuate(s, s % 2, False)
                    store(s, s % 2, slice(s * P, (s + 1) * P), 0)
                for n in range(QW, 2 * QW):
                    hi_w(n)
                with act.Fori(0, NB // 2) as i:
                    for p in range(2):
                        evacuate(NB + 2 * i + p, p, False)
                        store(NB + 2 * i + p, p, bass.ts(2 * i + p, P), 1)

            @block.vector
            def _(dve):
                def mean(s, p):
                    dve.wait_ge(s_sumsq, s + 1)
                    nc.vector.tensor_scalar(stat[:, p, 1:2], stat[:, p, 0:1], 1.0 / D, EPS, ALU.mult, ALU.add).then_inc(s_mean, 1)

                def normed(s, p):
                    dve.wait_ge(s_root, s + 1)
                    rms_chain(nc, dve, s_chain, CHAIN * s, stat[:, p, 1:2], stat[:, p, 2:3], stat[:, p, 3:4], stat[:, p, 4:5])
                    nc.vector.scalar_tensor_tensor(xt[:, p, :], xt[:, p, :], stat[:, p, 3:4], norm_row[:],
                                                   ALU.mult, ALU.mult).then_inc(s_h, 1)

                def stage_lo(s, p, first):
                    if not first:
                        dve.wait_ge(s_keep_lo, s - 1)
                    for q in range(2):
                        dve.wait_ge(s_hi, 2 * s + q + 1)
                        nc.vector.tensor_tensor(stg_lo[p][:, 4 * q:4 * q + 4, :].rearrange("p k t -> p (k t)"), tp[p][q][:],
                                                as_f32(stg_hi[p][:, 4 * q:4 * q + 4, :].rearrange("p k t -> p (k t)")),
                                                ALU.subtract).then_inc(s_lo, 1)

                def keep_hi(s, p, cols):
                    nc.vector.tensor_copy(hT_hi[:, :, cols], as_f32(stg_hi[p][:])).then_inc(s_keep_hi, 1)

                nc.vector.memset(zeros[:], 0.0).then_inc(s_zero, 1)
                dve.wait_ge(s_norm, 16)
                mean(0, 0)
                normed(0, 0)
                mean(1, 1)
                normed(1, 1)
                stage_lo(0, 0, True)
                keep_hi(0, 0, slice(0, P))
                mean(2, 0)
                normed(2, 0)
                stage_lo(1, 1, True)
                keep_hi(1, 1, slice(P, 2 * P))
                with dve.Fori(1, NB // 2 - 1) as i:
                    mean(2 * i + 1, 1)
                    normed(2 * i + 1, 1)
                    stage_lo(2 * i, 0, False)
                    keep_hi(2 * i, 0, bass.ts(2 * i, P))
                    mean(2 * i + 2, 0)
                    normed(2 * i + 2, 0)
                    stage_lo(2 * i + 1, 1, False)
                    keep_hi(2 * i + 1, 1, bass.ts(2 * i + 1, P))
                mean(NB - 1, 1)
                normed(NB - 1, 1)
                for s in (NB - 2, NB - 1):
                    stage_lo(s, s % 2, False)
                    keep_hi(s, s % 2, slice(s * P, (s + 1) * P))
                dve.wait_ge(s_keep_hi, NB)
                dve.wait_ge(s_keep_lo, NB)
                with dve.Fori(0, NB // 2) as i:
                    for p in range(2):
                        dve.wait_ge(s_v, NB + 2 * i + p - 1)
                        nc.vector.tensor_copy(stg_hi[p][:], as_f32(hT_hi[:, :, bass.ts(2 * i + p, P)]))
                        nc.vector.tensor_copy(stg_lo[p][:], as_f32(hT_lo[:, :, bass.ts(2 * i + p, P)])).then_inc(s_stage, 1)

            @block.tensor
            def _(pe):
                def transposes(s, p):
                    pe.wait_ge(s_h, s + 1)
                    for k in range(KT):
                        last = nc.tensor.transpose(tp[p][k // 4][:, (k % 4) * P:(k % 4 + 1) * P],
                                                   xt[:, p, k * P:(k + 1) * P], ident[:])
                    last.then_inc(s_tr, 1)

                def project(s, p, first, staged, count):
                    pe.wait_ge(staged, count)
                    if not first:
                        pe.wait_ge(s_vst, s - 1)
                    for k in range(KT):
                        for n, (a, b) in enumerate(((stg_hi, w_hi), (stg_hi, w_lo), (stg_lo, w_hi))):
                            last = nc.tensor.matmul(vp[p][:], a[p][:, k, :], b[:, k, :],
                                                    start=(k == 0 and n == 0), stop=(k == KT - 1 and n == 2))
                    last.then_inc(s_v, 1)

                pe.wait_ge(s_ident, 2)
                transposes(0, 0)
                transposes(1, 1)
                pe.wait_ge(s_wlo, QW)
                project(0, 0, True, s_lo, 2)
                transposes(2, 0)
                project(1, 1, True, s_lo, 4)
                with pe.Fori(1, NB // 2 - 1) as i:
                    transposes(2 * i + 1, 1)
                    project(2 * i, 0, False, s_lo, 4 * i + 2)
                    transposes(2 * i + 2, 0)
                    project(2 * i + 1, 1, False, s_lo, 4 * i + 4)
                transposes(NB - 1, 1)
                project(NB - 2, 0, False, s_lo, 2 * NB - 2)
                project(NB - 1, 1, False, s_lo, 2 * NB)
                pe.wait_ge(s_wlo, 2 * QW)
                with pe.Fori(0, NB // 2) as i:
                    for p in range(2):
                        project(NB + 2 * i + p, p, False, s_stage, 2 * i + p + 1)


def phase_qkg(nc, w_qkg, v_dram, qk_hi, qk_lo, g_dram, dv_dram, vb_dram, hT_hi, hT_lo):
    with ExitStack() as ctx:
        def sb(name, shape, dt):
            return ctx.enter_context(nc.sbuf_tensor(name, shape, dt))

        def sem(name):
            return ctx.enter_context(nc.semaphore(name))

        w_raw = sb("w_raw", [P, 2, KT, P], F32)
        w_hi = [sb(f"w_hi{p}", [P, KT, P], F32R) for p in range(2)]
        w_lo = [sb(f"w_lo{p}", [P, KT, P], F32R) for p in range(2)]
        out_hi = [sb(f"out_hi{p}", [P, NC, CH], F32) for p in range(2)]
        out_lo = [sb(f"out_lo{p}", [P, NC, CH], F32) for p in range(2)]
        va = sb("v_here", [P, D], F32)
        vb = sb("v_next", [P, D], F32)
        dv = sb("dv_parts", [P, H, 2, DH], F32R)
        pp = [[ctx.enter_context(nc.psum_tensor(f"proj_ps{p}{c}", [P, CH], F32)) for c in range(NC)] for p in range(2)]

        s_wraw = [sem(f"w_raw_loaded{p}") for p in range(2)]
        s_whi = sem("w_hi_ready")
        s_wlo = sem("w_lo_ready")
        s_pp = sem("projection_ready")
        s_ohi = sem("out_hi_ready")
        s_olo = sem("out_lo_ready")
        s_out = [sem(f"tile_stored{p}") for p in range(2)]
        s_passed = sem("waits_passed_qkg")
        s_va = sem("v_loaded")
        s_dif = sem("dv_ready")
        s_dhi = sem("dv_hi_ready")
        s_dlo = sem("dv_lo_ready")
        s_dout = sem("dv_stored")

        NT = 3 * KT
        NQK = 2 * KT

        with nc.Block() as block:
            @block.sync
            def _(sp):
                for p in range(2):
                    sp.dma_start(w_raw[:, p, :, :], w_qkg[p]).then_inc(s_wraw[p], 16)
                sp.dma_start(va[0:NB, :], v_dram[0:S, :].rearrange("(b p) n -> b p n", p=P)[:, 0, :]).then_inc(s_va, 16)
                sp.wait_ge(s_dlo, 1)
                sp.dma_start(vb_dram[:], as_f32(dv[0:NB]).rearrange("b h a n -> b (h a n)")).then_inc(s_dout, 16)
                sp.dma_start(va[:], v_dram[0:P, :]).then_inc(s_va, 16)
                sp.dma_start(vb[:], v_dram[1:P + 1, :]).then_inc(s_va, 16)

                def load_dv(t):
                    sp.dma_start(va[:], v_dram[bass.ds(t * P, P), :]).then_inc(s_va, 16)
                    sp.dma_start(vb[:], v_dram[bass.ds(t * P + 1, P), :]).then_inc(s_va, 16)

                def store_dv(t):
                    sp.wait_ge(s_dlo, t + 2)
                    pass_waits(sp, s_passed)
                    sp.dma_start(dv_dram[:, :, t, :].rearrange("h p n -> p h n"),
                                 as_f32(dv[:]).rearrange("p h a n -> p h (a n)")).then_inc(s_dout, 16)

                def load(t, p):
                    sp.wait_ge(s_wlo, t + 1)
                    sp.dma_start(w_raw[:, p, :, :], w_qkg[t + 2]).then_inc(s_wraw[p], 16)

                def store(t, p):
                    rows = bass.ds(t * P, P)
                    sp.wait_ge(s_olo, NC * (t + 1))
                    sp.dma_start(qk_hi[rows, :], out_hi[p][:].rearrange("p c n -> p (c n)")).then_inc(s_out[p], 16)
                    sp.dma_start(qk_lo[rows, :], out_lo[p][:].rearrange("p c n -> p (c n)")).then_inc(s_out[p], 16)

                def store_gate(t, p):
                    sp.wait_ge(s_olo, NC * (t + 1))
                    sp.dma_start(g_dram[bass.ds((t - NQK) * P, P), :],
                                 out_lo[p][:].rearrange("p c n -> p (c n)")).then_inc(s_out[p], 16)

                with sp.Fori(0, NQK // 2 - 1) as i:
                    for p in range(2):
                        load(2 * i + p, p)
                        store_dv(2 * i + p)
                        load_dv(2 * i + p + 1)
                        store(2 * i + p, p)
                for p in range(2):
                    load(NQK - 2 + p, p)
                    store_dv(NQK - 2 + p)
                    if p == 0:
                        load_dv(NQK - 1)
                    store(NQK - 2 + p, p)
                with sp.Fori(NQK // 2, NT // 2 - 1) as i:
                    for p in range(2):
                        load(2 * i + p, p)
                        store_gate(2 * i + p, p)
                for p in range(2):
                    store_gate(NT - 2 + p, p)
                for p in range(2):
                    sp.wait_ge(s_out[p], 16 * NQK + 8 * (NT - NQK))
                sp.wait_ge(s_dout, 16 * (NB + 1))

            @block.gpsimd
            def _(pool):
                def split(t, p, first):
                    pool.wait_ge(s_wraw[p], 8 * (t - p) + 16)
                    if not first:
                        pool.wait_ge(s_pp, NC * (t - 1))
                    pass_waits(pool, s_passed)
                    nc.gpsimd.tensor_copy(w_hi[p][:], w_raw[:, p, :, :]).then_inc(s_whi, 1)
                    pool.wait_ge(s_whi, t + 1)
                    nc.gpsimd.tensor_tensor(w_lo[p][:], w_raw[:, p, :, :], as_f32(w_hi[p][:]), ALU.subtract).then_inc(s_wlo, 1)
                for p in range(2):
                    split(p, p, True)
                with pool.Fori(1, NT // 2) as i:
                    for p in range(2):
                        split(2 * i + p, p, False)

            @block.tensor
            def _(pe):
                def tile(t, p, first):
                    pe.wait_ge(s_wlo, t + 1)
                    for c in range(NC):
                        if not first:
                            pe.wait_ge(s_olo, NC * (t - 2) + c + 1)
                        cols = slice(c * CH, (c + 1) * CH)
                        for k in range(KT):
                            for n, (a, b) in enumerate(((w_hi, hT_hi), (w_hi, hT_lo), (w_lo, hT_hi))):
                                last = nc.tensor.matmul(pp[p][c][:], a[p][:, k, :], b[:, k, cols],
                                                        start=(k == 0 and n == 0), stop=(k == KT - 1 and n == 2))
                        last.then_inc(s_pp, 1)
                for p in range(2):
                    tile(p, p, True)
                with pe.Fori(1, NT // 2) as i:
                    for p in range(2):
                        tile(2 * i + p, p, False)

            @block.scalar
            def _(act):
                def dv_hi(t, rows=P):
                    nc.scalar.activation(dv[0:rows, :, 0, :], va[0:rows, :].rearrange("p (h n) -> p h n", h=H),
                                         ACT.Copy).then_inc(s_dhi, 1)

                def tile_hi(t, p, first, func, stores):
                    def out(c):
                        return out_hi[p][:, c, :].bitcast(F32R) if func == ACT.Copy else out_hi[p][:, c, :]
                    if not first:
                        act.wait_ge(s_out[p], stores)
                    for c in range(NC):
                        act.wait_ge(s_pp, NC * t + c + 1)
                        nc.scalar.activation(out(c), pp[p][c][:], func).then_inc(s_ohi, 1)
                def dv_hi_of(t):
                    act.wait_ge(s_dif, t + 1)
                    act.wait_ge(s_dout, 16 * (t + 1))
                    dv_hi(t)

                act.wait_ge(s_va, 16)
                dv_hi(-1, NB)
                for p in range(2):
                    dv_hi_of(p)
                    tile_hi(p, p, True, ACT.Copy, None)
                with act.Fori(1, NQK // 2) as i:
                    for p in range(2):
                        dv_hi_of(2 * i + p)
                        tile_hi(2 * i + p, p, False, ACT.Copy, 32 * i)
                with act.Fori(NQK // 2, NT // 2) as i:
                    for p in range(2):
                        tile_hi(2 * i + p, p, False, ACT.Sigmoid, 16 * i + 16 * NQK // 2)

            @block.vector
            def _(dve):
                def dv_lo(t, rows=P):
                    dve.wait_ge(s_dhi, t + 2)
                    nc.vector.tensor_tensor(dv[0:rows, :, 1, :], va[0:rows, :].rearrange("p (h n) -> p h n", h=H),
                                            as_f32(dv[0:rows, :, 0, :]), ALU.subtract).then_inc(s_dlo, 1)

                def dif(t):
                    dve.wait_ge(s_va, 32 * (t + 1) + 16)
                    nc.vector.tensor_tensor(va[:], vb[:], va[:], ALU.subtract).then_inc(s_dif, 1)

                def tile_lo(t, p, op, stores, first):
                    if not first:
                        dve.wait_ge(s_out[p], stores)
                    for c in range(NC):
                        dve.wait_ge(s_ohi, NC * t + c + 1)
                        nc.vector.tensor_tensor(out_lo[p][:, c, :], pp[p][c][:], out_hi[p][:, c, :], op).then_inc(s_olo, 1)
                dv_lo(-1, NB)
                for p in range(2):
                    dif(p)
                    dv_lo(p)
                    tile_lo(p, p, ALU.subtract, None, True)
                with dve.Fori(1, NQK // 2) as i:
                    for p in range(2):
                        dif(2 * i + p)
                        dv_lo(2 * i + p)
                        tile_lo(2 * i + p, p, ALU.subtract, 32 * i, False)
                with dve.Fori(NQK // 2, NT // 2) as i:
                    for p in range(2):
                        tile_lo(2 * i + p, p, ALU.mult, 16 * i + 16 * NQK // 2, False)


def head_steps():
    return [(c, j, r) for c in range(NC) for j in range(c, NC) for r in range(CB)]


STEPS = head_steps()
HS = len(STEPS)
PAIR = 2 * HS
LEAD_SCORES = 8
LEAD_SCAN = 6
LEAD_TURN = 3
RU, RZ, RT, RO = 4, 2, 4, 2


def phase_attention(nc, qk_hi, qk_lo, dv_dram, vb_dram, w_out, o_hi, o_lo, wo_hi, wo_lo, ident):
    with ExitStack() as ctx:
        def sb(name, shape, dt):
            return ctx.enter_context(nc.sbuf_tensor(name, shape, dt))

        def pb(name):
            return ctx.enter_context(nc.psum_tensor(name, [P, CH], F32))

        def sem(name):
            return ctx.enter_context(nc.semaphore(name))

        q_t = [sb(f"q_parts{p}", [P, S], F32R) for p in range(2)]
        kh_t = [sb(f"k_hi_twice{p}", [P, S], F32R) for p in range(2)]
        kl_t = [sb(f"k_lo_twice{p}", [P, S], F32R) for p in range(2)]
        dv_t = [sb(f"dv_head{p}", [P, NB, P], F32R) for p in range(2)]
        vb_t = [sb(f"v_first{p}", [NB, P], F32R) for p in range(2)]
        block_of = sb("block_of_token", [NB, S], F32R)
        u_t = [[sb(f"u{n}_{r}", [P, CH], F32) for r in range(CB)] for n in range(RU)]
        rt_hi = [sb(f"r_turned_hi{n}", [P, CH], F32R) for n in range(RT)]
        rt_lo = [sb(f"r_turned_lo{n}", [P, CH], F32R) for n in range(RT)]
        o_st = [sb(f"o_stage{n}", [P, CH], F32) for n in range(RO)]
        wo_raw = sb("w_out_raw", [P, D], F32)
        ident_b = sb("ident_bf16", [P, P], BF16)
        mask_b = sb("mask_bf16", [P, P], BF16)
        z_ps = [pb(f"z_ps{n}") for n in range(RZ)]
        t_ps = [pb(f"turn_ps{n}") for n in range(RT)]
        o_ps = [pb(f"o_ps{n}") for n in range(RO)]

        s_qk = [sem(f"qk_loaded{p}") for p in range(2)]
        s_dv = [sem(f"dv_loaded{p}") for p in range(2)]
        s_const = sem("constants_ready")
        s_z = sem("scores_ready")
        s_u = sem("u_ready")
        s_r = sem("scan_ready")
        s_t = sem("turned")
        s_hi = sem("r_hi_ready")
        s_lo = sem("r_lo_ready")
        s_o = sem("o_ready")
        s_ost = sem("o_evacuated")
        s_oout = [sem(f"o_stored{n}") for n in range(2)]
        s_passed = sem("waits_passed_attention")
        s_woraw = sem("w_out_raw_loaded")
        s_wohi = sem("w_out_hi_ready")
        s_wolo = sem("w_out_lo_ready")

        NLOAD = 6 * 16

        def score_cols(m):
            c, j, r = STEPS[m % HS]
            return r * P if j == c else 0

        def turn_width(m):
            c, j, r = STEPS[m % HS]
            return (r + 1) * P if j == c else CH

        with nc.Block() as block:
            @block.sync
            def _(sp):
                def load(h, p):
                    rows = bass.ds(h * DH, DH)
                    krows = bass.ds(h * DH + D, DH)
                    for half in range(2):
                        part = slice(half * DH, (half + 1) * DH)
                        sp.dma_start(as_f32(q_t[p][part, :]), (qk_hi, qk_lo)[half][rows, :]).then_inc(s_qk[p], 16)
                        sp.dma_start(as_f32(kh_t[p][part, :]), qk_hi[krows, :]).then_inc(s_qk[p], 16)
                        sp.dma_start(as_f32(kl_t[p][part, :]), qk_lo[krows, :]).then_inc(s_qk[p], 16)
                    sp.dma_start(as_f32(dv_t[p][:]), dv_dram[h]).then_inc(s_dv[p], 16)
                    sp.dma_start(as_f32(vb_t[p][:]), vb_dram[:, bass.ds(h * P, P)]).then_inc(s_dv[p], 16)
                for p in range(2):
                    load(p, p)

                def store(pairs, g):
                    c, p = g % NC, g // NC
                    sp.wait_ge(s_ost, NC * 2 * pairs + g + 1)
                    pass_waits(sp, s_passed)
                    rows = bass.ds((2 * pairs + p) * DH, DH)
                    sp.dma_start(o_hi[rows, c * CH:(c + 1) * CH], o_st[c % RO][0:DH, :]).then_inc(s_oout[c % RO], 16)
                    sp.dma_start(o_lo[rows, c * CH:(c + 1) * CH], o_st[c % RO][DH:P, :]).then_inc(s_oout[c % RO], 16)

                with sp.Fori(0, H // 2 - 1) as i:
                    for p in range(2):
                        for c in range(NC):
                            store(i, NC * p + c)
                        load(2 * i + 2 + p, p)
                for g in range(2 * NC):
                    store(H // 2 - 1, g)
                for n in range(2):
                    sp.wait_ge(s_oout[n], 32 * H * NC // 2)

            @block.gpsimd
            def _(pool):
                tmp = as_f32(block_of[:])
                nc.gpsimd.memset(ident_b[:], 0.0).then_inc(s_const, 1)
                nc.gpsimd.memset(mask_b[:], MASKED).then_inc(s_const, 1)
                nc.gpsimd.memset(tmp, 1.0).then_inc(s_const, 1)
                pool.wait_ge(s_const, 3)
                nc.gpsimd.affine_select(out=ident_b[:], in_=ident_b[:], compare_op=ALU.not_equal, fill=1.0, base=0,
                                        pattern=[[-1, P]], channel_multiplier=1).then_inc(s_const, 1)
                nc.gpsimd.affine_select(out=mask_b[:], in_=mask_b[:], compare_op=ALU.is_ge, fill=0.0, base=0,
                                        pattern=[[-1, P]], channel_multiplier=1).then_inc(s_const, 1)
                nc.gpsimd.affine_select(out=block_of[:], in_=tmp, compare_op=ALU.is_ge, fill=0.0, base=0,
                                        pattern=[[1, S]], channel_multiplier=-P).then_inc(s_const, 1)
                pool.wait_ge(s_const, 6)
                nc.gpsimd.affine_select(out=block_of[:], in_=tmp, compare_op=ALU.is_ge, fill=0.0, base=P - 1,
                                        pattern=[[-1, S]], channel_multiplier=P).then_inc(s_const, 1)
                for k in range(KT):
                    if k:
                        pool.wait_ge(s_wolo, k)
                    pool.dma_start(wo_raw[:], w_out[k * P:(k + 1) * P, :]).then_inc(s_woraw, 16)
                    pool.wait_ge(s_woraw, 16 * (k + 1))
                    nc.gpsimd.tensor_copy(wo_hi[:, k, :], wo_raw[:]).then_inc(s_wohi, 1)
                    pool.wait_ge(s_wohi, k + 1)
                    nc.gpsimd.tensor_tensor(wo_lo[:, k, :], wo_raw[:], as_f32(wo_hi[:, k, :]), ALU.subtract).then_inc(s_wolo, 1)


            def over_pairs(eng, body):
                body(0, True, False)
                with eng.Fori(1, H // 2 - 1) as i:
                    body(i * PAIR, False, False)
                body((H // 2 - 1) * PAIR, False, True)

            @block.tensor
            def _(pe):
                def scores(at, m):
                    p, (c, j, r) = (m // HS) % 2, STEPS[m % HS]
                    lo = score_cols(m)
                    tau = slice(c * CH + r * P, c * CH + (r + 1) * P)
                    sig = slice(j * CH + lo, (j + 1) * CH)
                    out = z_ps[m % RZ][:, 0:CH - lo]
                    nc.tensor.matmul(out, q_t[p][:, tau], kh_t[p][:, sig], start=True, stop=False)
                    last = nc.tensor.matmul(out, q_t[p][:, tau], kl_t[p][:, sig], start=False, stop=(j != c))
                    if j == c:
                        last = nc.tensor.matmul(out[:, 0:P], ident_b[:], mask_b[:], start=False, stop=True)
                    last.then_inc(s_z, 1)

                def scores_waits(at, m):
                    if m % HS == 0:
                        pe.wait_ge(s_qk[(m // HS) % 2], NLOAD * (at // PAIR + m // PAIR + 1))
                    pe.wait_ge(s_u, at + m - RZ + 1)

                def turn(m):
                    c, j, r = STEPS[m % HS]
                    unit = (m // CB) % RU
                    for t in range(turn_width(m) // P):
                        lo = t * P if j == c else 0
                        last = nc.tensor.transpose(t_ps[m % RT][:, t * P:(t + 1) * P],
                                                   u_t[unit][t][:, r * P - lo:(r + 1) * P - lo], ident[:])
                    last.then_inc(s_t, 1)

                def weigh(m):
                    p, (c, j, r) = (m // HS) % 2, STEPS[m % HS]
                    w = turn_width(m)
                    out = o_ps[c % RO]
                    if j == c and r == 0:
                        nc.tensor.matmul(out[:], vb_t[p][:], block_of[:, c * CH:(c + 1) * CH], start=True, stop=False)
                    end = j == NC - 1 and r == CB - 1
                    weights = dv_t[p][:, j * CB + r, :]
                    nc.tensor.matmul(out[:, 0:w], weights, rt_hi[m % RT][:, 0:w], start=False, stop=False)
                    last = nc.tensor.matmul(out[:, 0:w], weights, rt_lo[m % RT][:, 0:w], start=False, stop=end)
                    if end:
                        last.then_inc(s_o, 1)

                pe.wait_ge(s_const, 7)
                pe.wait_ge(s_qk[0], NLOAD)
                for m in range(LEAD_SCORES):
                    if m >= RZ:
                        pe.wait_ge(s_u, m - RZ + 1)
                    scores(0, m)
                pe.wait_ge(s_r, LEAD_TURN)
                for m in range(LEAD_TURN):
                    turn(m)

                def pair(at, first, last):
                    for n in range(PAIR):
                        if n % HS == 0:
                            pe.wait_ge(s_dv[n // HS], 32 * (at // PAIR + 1))
                        if n + LEAD_SCORES < PAIR or not last:
                            scores_waits(at, n + LEAD_SCORES)
                            scores(at, n + LEAD_SCORES)
                        pe.wait_ge(s_lo, at + n + 1)
                        weigh(n)
                        if n + LEAD_TURN < PAIR or not last:
                            turn(n + LEAD_TURN)
                over_pairs(pe, pair)

            @block.scalar
            def _(act):
                def stick(at, m):
                    w = CH - score_cols(m)
                    act.wait_ge(s_z, at + m + 1)
                    nc.scalar.activation(u_t[(m // CB) % RU][STEPS[m % HS][2]][:, 0:w], z_ps[m % RZ][:, 0:w],
                                         ACT.Sigmoid, scale=-Z_SCALE).then_inc(s_u, 1)

                def hi(at, m):
                    w = turn_width(m)
                    act.wait_ge(s_t, at + m + 1)
                    nc.scalar.activation(rt_hi[m % RT][:, 0:w], t_ps[m % RT][:, 0:w], ACT.Copy).then_inc(s_hi, 1)

                def chunk_end(m):
                    c, j, r = STEPS[m % HS]
                    return NC * (m // HS) + c if j == NC - 1 and r == CB - 1 else None

                def empty(at, g, first):
                    c, pairs = g % NC, at // PAIR
                    act.wait_ge(s_o, NC * 2 * pairs + g + 1)
                    if not (first and g < RO):
                        act.wait_ge(s_oout[c % RO], 32 * (NC * pairs + g // RO))
                    nc.scalar.activation(o_st[c % RO][:], o_ps[c % RO][:], ACT.Copy).then_inc(s_ost, 1)

                for m in range(LEAD_SCAN):
                    stick(0, m)
                for m in range(LEAD_TURN):
                    stick(0, m + LEAD_SCAN)
                    hi(0, m)

                def pair(at, first, last):
                    for m in range(LEAD_TURN, PAIR + LEAD_TURN):
                        if m + LEAD_SCAN < PAIR or not last:
                            stick(at, m + LEAD_SCAN)
                        done = chunk_end(m - LEAD_TURN)
                        if done is not None:
                            empty(at, done, first)
                        if m < PAIR or not last:
                            hi(at, m)
                over_pairs(act, pair)

            @block.vector
            def _(dve):
                def scan(at, m):
                    c, j, r = STEPS[m % HS]
                    u = u_t[(m // CB) % RU][r][:, 0:CH - score_cols(m)]
                    if j == c:
                        start = 1.0
                    else:
                        w = CH - score_cols(m - CB)
                        start = u_t[(m // CB - 1) % RU][r][:, w - 1:w]
                        dve.wait_ge(s_r, at + m - CB + 1)
                    dve.wait_ge(s_u, at + m + 1)
                    nc.vector.tensor_tensor_scan(u, u, u, start, ALU.mult, ALU.min).then_inc(s_r, 1)

                def lo(at, m):
                    w = turn_width(m)
                    dve.wait_ge(s_hi, at + m + 1)
                    nc.vector.tensor_tensor(rt_lo[m % RT][:, 0:w], t_ps[m % RT][:, 0:w],
                                            as_f32(rt_hi[m % RT][:, 0:w]), ALU.subtract).then_inc(s_lo, 1)

                for m in range(LEAD_SCAN):
                    scan(0, m)

                def pair(at, first, last):
                    for m in range(PAIR):
                        if m + LEAD_SCAN < PAIR or not last:
                            scan(at, m + LEAD_SCAN)
                        lo(at, m)
                over_pairs(dve, pair)


def phase_output(nc, x, final_norm, o_hi, o_lo, g_dram, out, wo_hi, wo_lo):
    with ExitStack() as ctx:
        def sb(name, shape, dt):
            return ctx.enter_context(nc.sbuf_tensor(name, shape, dt))

        def sem(name):
            return ctx.enter_context(nc.semaphore(name))

        GB = 2
        GT = GB * P
        NG = S // GT
        oa = sb("o_part_hi", [P, 2, KT, GT], F32)
        ob = sb("o_part_lo", [P, 2, KT, GT], F32)
        gt = sb("gate", [P, 2, KT, GT], F32)
        m_hi = [sb(f"gated_hi{p}", [P, KT, GT], F32R) for p in range(2)]
        m_lo = [sb(f"gated_lo{p}", [P, KT, GT], F32R) for p in range(2)]
        xt = sb("x_again", [P, GB, D], F32)
        norm_row = sb("final_norm_row", [P, D], F32)
        junk = sb("square_junk2", [P, D], BF16)
        stat = sb("stat2", [P, GB, 5], F32)
        yp = [[[ctx.enter_context(nc.psum_tensor(f"y_ps{p}{b}{f}", [P, CH], F32)) for f in range(2)]
               for b in range(GB)] for p in range(2)]

        s_norm = sem("final_norm_loaded")
        s_in = [sem(f"group_loaded{p}") for p in range(2)]
        s_x = [sem(f"x_again_loaded{b}") for b in range(GB)]
        s_sum = sem("o_parts_added")
        s_gated = sem("gated")
        s_mhi = sem("gated_hi_ready")
        s_mlo = sem("gated_lo_ready")
        s_y = sem("y_ready")
        s_res = sem("residual_added")
        s_sumsq = sem("y_sum_squares")
        s_mean = sem("y_mean_square")
        s_root = sem("y_root")
        s_chain = sem("y_rms_chain")
        s_out = sem("out_ready")
        s_stored = [sem(f"out_stored{b}") for b in range(GB)]

        with nc.Block() as block:
            @block.sync
            def _(sp):
                sp.dma_start(norm_row[:], final_norm.rearrange("(a n) -> a n", a=1).to_broadcast([P, D])).then_inc(s_norm, 16)

                def load(t, p):
                    for tile, src in ((oa, o_hi), (ob, o_lo), (gt, g_dram)):
                        sp.dma_start(tile[:, p, :, :],
                                     src.rearrange("(k p) t -> p k t", p=P)[:, :, bass.ds(t * GT, GT)]).then_inc(s_in[p], 16)

                def load_x(t, b, first):
                    if not first:
                        sp.wait_ge(s_stored[b], 16 * t)
                    sp.dma_start(xt[:, b, :], x[bass.ds(t * GT + b * P, P), :]).then_inc(s_x[b], 16)
                for p in range(2):
                    load(p, p)
                for b in range(GB):
                    load_x(0, b, True)
                with sp.Fori(0, NG // 2 - 1) as i:
                    for p in range(2):
                        t = 2 * i + p
                        sp.wait_ge(s_mlo, t + 1)
                        load(t + 2, p)
                        for b in range(GB):
                            load_x(t + 1, b, False)
                for b in range(GB):
                    load_x(NG - 1, b, False)
                for b in range(GB):
                    sp.wait_ge(s_stored[b], 16 * NG)

            @block.tensor
            def _(pe):
                def group(t, p, first):
                    pe.wait_ge(s_mlo, t + 1)
                    for b in range(GB):
                        if not first:
                            pe.wait_ge(s_res, GB * (t - 2) + b + 1)
                        tok = slice(b * P, (b + 1) * P)
                        for f in range(2):
                            cols = slice(f * CH, (f + 1) * CH)
                            for k in range(KT):
                                for n, (a, w) in enumerate(((m_hi, wo_hi), (m_hi, wo_lo), (m_lo, wo_hi))):
                                    last = nc.tensor.matmul(yp[p][b][f][:], a[p][:, k, tok], w[:, k, cols],
                                                            start=(k == 0 and n == 0), stop=(k == KT - 1 and n == 2))
                        last.then_inc(s_y, 1)
                for p in range(2):
                    group(p, p, True)
                with pe.Fori(1, NG // 2) as i:
                    for p in range(2):
                        group(2 * i + p, p, False)

            @block.vector
            def _(dve):
                def gate(t, p, first):
                    dve.wait_ge(s_in[p], 24 * (t - p) + 48)
                    nc.vector.tensor_tensor(oa[:, p], oa[:, p], ob[:, p], ALU.add).then_inc(s_sum, 1)
                    dve.wait_ge(s_sum, t + 1)
                    nc.vector.tensor_tensor(oa[:, p], oa[:, p], gt[:, p], ALU.mult).then_inc(s_gated, 1)
                    dve.wait_ge(s_mhi, t + 1)
                    nc.vector.tensor_tensor(m_lo[p][:], oa[:, p], as_f32(m_hi[p][:]), ALU.subtract).then_inc(s_mlo, 1)

                def finish(t, p, b):
                    n = GB * t + b
                    dve.wait_ge(s_y, n + 1)
                    dve.wait_ge(s_x[b], 16 * (t + 1))
                    for f in range(2):
                        cols = slice(f * CH, (f + 1) * CH)
                        last = nc.vector.tensor_tensor(xt[:, b, cols], yp[p][b][f][:], xt[:, b, cols], ALU.add)
                    last.then_inc(s_res, 1)
                    dve.wait_ge(s_sumsq, n + 1)
                    nc.vector.tensor_scalar(stat[:, b, 1:2], stat[:, b, 0:1], 1.0 / D, EPS, ALU.mult, ALU.add).then_inc(s_mean, 1)
                    dve.wait_ge(s_root, n + 1)
                    rms_chain(nc, dve, s_chain, CHAIN * n, stat[:, b, 1:2], stat[:, b, 2:3], stat[:, b, 3:4], stat[:, b, 4:5])
                    nc.vector.scalar_tensor_tensor(xt[:, b, :], xt[:, b, :], stat[:, b, 3:4], norm_row[:],
                                                   ALU.mult, ALU.mult).then_inc(s_out, 1)

                dve.wait_ge(s_norm, 16)
                gate(0, 0, True)
                gate(1, 1, True)
                for b in range(GB):
                    finish(0, 0, b)
                with dve.Fori(0, NG // 2 - 1) as i:
                    gate(2 * i + 2, 0, False)
                    for b in range(GB):
                        finish(2 * i + 1, 1, b)
                    gate(2 * i + 3, 1, False)
                    for b in range(GB):
                        finish(2 * i + 2, 0, b)
                for b in range(GB):
                    finish(NG - 1, 1, b)

            @block.scalar
            def _(act):
                def hi(t, p):
                    act.wait_ge(s_gated, t + 1)
                    nc.scalar.activation(m_hi[p][:], oa[:, p], ACT.Copy).then_inc(s_mhi, 1)

                def finish(t, b, first=False):
                    n = GB * t + b
                    act.wait_ge(s_res, n + 1)
                    if not first:
                        act.wait_ge(s_sumsq, n)
                    nc.scalar.activation(junk[:], xt[:, b, :], ACT.Square, accum_out=stat[:, b, 0:1]).then_inc(s_sumsq, 1)
                    act.wait_ge(s_mean, n + 1)
                    nc.scalar.activation(stat[:, b, 2:3], stat[:, b, 1:2], ACT.Sqrt).then_inc(s_root, 1)
                    act.wait_ge(s_out, n + 1)
                    act.dma_start(out[bass.ds(t * GT + b * P, P), :], xt[:, b, :]).then_inc(s_stored[b], 16)

                hi(0, 0)
                hi(1, 1)
                for b in range(GB):
                    finish(0, b, first=(b == 0))
                with act.Fori(0, NG // 2 - 1) as i:
                    act.wait_ge(s_y, 2 * GB * i + GB)
                    hi(2 * i + 2, 0)
                    for b in range(GB):
                        finish(2 * i + 1, b)
                    hi(2 * i + 3, 1)
                    for b in range(GB):
                        finish(2 * i + 2, b)
                for b in range(GB):
                    finish(NG - 1, b)


def stick_breaking_layer(nc, x, a_norm, w_v, w_qkg, w_out, final_norm, out):
    def scratch(name, shape, dt):
        return nc.dram_tensor(name, shape, dt, kind="Internal").ap()

    v_dram = scratch("v_rows", [S + 1, D], F32)
    qk_hi = scratch("qk_hi_cols", [2 * D, S], F32)
    qk_lo = scratch("qk_lo_cols", [2 * D, S], F32)
    g_dram = scratch("gate_cols", [D, S], F32)
    dv_dram = scratch("dv_parts_dram", [H, P, NB, P], F32)
    vb_dram = scratch("v_first_dram", [NB, H * P], F32)
    o_hi = scratch("o_hi_cols", [D, S], F32)
    o_lo = scratch("o_lo_cols", [D, S], F32)

    with ExitStack() as ctx:
        ident = ctx.enter_context(nc.sbuf_tensor("ident", [P, P], F32))
        with ExitStack() as projections:
            hT_hi = projections.enter_context(nc.sbuf_tensor("hT_hi", [P, KT, S], F32R))
            hT_lo = projections.enter_context(nc.sbuf_tensor("hT_lo", [P, KT, S], F32R))
            phase_norm_and_v(nc, x, a_norm, w_v, v_dram, hT_hi, hT_lo, ident)
            phase_qkg(nc, w_qkg, v_dram, qk_hi, qk_lo, g_dram, dv_dram, vb_dram, hT_hi, hT_lo)
        wo_hi = ctx.enter_context(nc.sbuf_tensor("wo_hi", [P, KT, D], F32R))
        wo_lo = ctx.enter_context(nc.sbuf_tensor("wo_lo", [P, KT, D], F32R))
        phase_attention(nc, qk_hi, qk_lo, dv_dram, vb_dram, w_out, o_hi, o_lo, wo_hi, wo_lo, ident)
        phase_output(nc, x, final_norm, o_hi, o_lo, g_dram, out, wo_hi, wo_lo)


def kernel(**inputs):
    import numpy as np
    import concourse.bacc as bacc
    from concourse.bass_utils import run_bass_kernel_spmd

    w_in = np.asarray(inputs["a_w_in"])[0]
    w_v = w_in[:, 2 * D:3 * D].reshape(KT, P, D // CH, CH).transpose(2, 1, 0, 3)
    w_qkg = np.concatenate([w_in[:, :2 * D], w_in[:, 3 * D:]], axis=1).reshape(KT, P, 3 * KT, P).transpose(2, 1, 0, 3)
    arrays = {
        "in_x": np.ascontiguousarray(np.asarray(inputs["x"])[0, ::-1]),
        "in_a_norm": np.ascontiguousarray(np.asarray(inputs["a_norm"])[0]),
        "in_w_v": np.ascontiguousarray(w_v),
        "in_w_qkg": np.ascontiguousarray(w_qkg),
        "in_w_out": np.ascontiguousarray(np.asarray(inputs["a_w_out"])[0]),
        "in_final_norm": np.ascontiguousarray(np.asarray(inputs["final_norm"])),
    }
    nc = bacc.Bacc("TRN2", target_bir_lowering=False, num_devices=1)
    args = [nc.dram_tensor(name, a.shape, mybir.dt.from_np(a.dtype), kind="ExternalInput").ap() for name, a in arrays.items()]
    out = nc.dram_tensor("out", (S, D), F32, kind="ExternalOutput").ap()
    stick_breaking_layer(nc, *args, out)
    result = run_bass_kernel_spmd(nc, [arrays], core_ids=[0]).results[0]["out"]
    return np.ascontiguousarray(result[::-1])[None]
```

```python
import concourse.bass as bass
from concourse import mybir
from contextlib import ExitStack

F32 = mybir.dt.float32
F32R = mybir.dt.float32r
BF16 = mybir.dt.bfloat16
ALU = mybir.AluOpType
ACT = mybir.ActivationFunctionType

P = 128
S = 2048
D = 1024
H = 16
DH = D // H
KT = D // P
NB = S // P
CH = 512
NC = S // CH
CB = CH // P
EPS = 1e-6
Z_SCALE = DH ** -0.5


def as_f32(ap):
    return ap.bitcast(F32)


def pass_waits(eng, passed):
    eng.sem_inc(passed, 1)


def rms_chain(nc, dve, chain, count, mean_sq, root, recip, tmp):
    def link(ins):
        nonlocal count
        ins.then_inc(chain, 1)
        count = count + 1
        dve.wait_ge(chain, count)
    link(nc.vector.reciprocal(recip, root))
    link(nc.vector.tensor_tensor(tmp, recip, recip, ALU.mult))
    link(nc.vector.tensor_tensor(tmp, tmp, mean_sq, ALU.mult))
    link(nc.vector.tensor_scalar(tmp, tmp, -0.5, 1.5, ALU.mult, ALU.add))
    link(nc.vector.tensor_tensor(recip, recip, tmp, ALU.mult))
    return count


CHAIN = 5


def phase_norm_and_v(nc, x, a_norm, w_v, w_qkg, v_dram, hT_hi, hT_lo, ident, raw, s_tile):
    with ExitStack() as ctx:
        def sb(name, shape, dt):
            return ctx.enter_context(nc.sbuf_tensor(name, shape, dt))

        def pb(name):
            return ctx.enter_context(nc.psum_tensor(name, [P, CH], F32))

        def sem(name):
            return ctx.enter_context(nc.semaphore(name))

        w_raw = raw[:].rearrange("p a (k n) -> p a k n", k=2)
        w_hi = sb("wv_hi", [P, KT, CH], F32R)
        w_lo = sb("wv_lo", [P, KT, CH], F32R)
        xt = sb("xt", [P, 2, D], F32)
        norm_row = sb("a_norm_row", [P, D], F32)
        junk = sb("square_junk", [P, D], BF16)
        stg_hi = [sb(f"stage_hi{p}", [P, KT, P], F32R) for p in range(2)]
        stg_lo = [sb(f"stage_lo{p}", [P, KT, P], F32R) for p in range(2)]
        vst = sb("v_stage", [P, 2, CH], F32)
        stat = sb("stat", [P, 2, 5], F32)
        zeros = sb("zeros", [D // CH, CH], F32)
        tp = [[pb(f"hT_ps{p}{q}") for q in range(2)] for p in range(2)]
        vp = [pb(f"v_ps{p}") for p in range(2)]

        s_ident = sem("ident_ready")
        s_norm = sem("norm_row_loaded")
        s_x = [sem(f"x_loaded{p}") for p in range(2)]
        s_wraw = [sem(f"wv_raw_loaded{p}") for p in range(2)]
        s_wused = sem("wv_quarter_used")
        s_whi = sem("wv_hi_ready")
        s_wlo = sem("wv_lo_ready")
        s_sumsq = sem("sum_squares_ready")
        s_mean = sem("mean_square_ready")
        s_root = sem("root_ready")
        s_chain = sem("rms_chain")
        s_h = sem("h_ready")
        s_tr = sem("h_transposed")
        s_hi = sem("stage_hi_ready")
        s_lo = sem("stage_lo_ready")
        s_keep_hi = sem("hT_hi_kept")
        s_keep_lo = sem("hT_lo_kept")
        s_v = sem("v_ready")
        s_vst = sem("v_evacuated")
        s_vout = [sem(f"v_stored{p}") for p in range(2)]
        s_stage = sem("stage_reloaded")
        s_passed = sem("waits_passed_norm")
        s_zero = sem("zero_row")
        s_zout = sem("zero_row_stored")

        NPASS = 2
        QW = KT // 2
        quarter = [slice(2 * q, 2 * q + 2) for q in range(QW)]

        with nc.Block() as block:
            @block.sync
            def _(sp):
                sp.dma_start(norm_row[:], a_norm.rearrange("(a n) -> a n", a=1).to_broadcast([P, D])).then_inc(s_norm, 16)
                sp.dma_start(xt[:, 0, :], x[0:P, :]).then_inc(s_x[0], 16)

                def load_w(n):
                    half, q = n // QW, n % QW
                    if n >= 2:
                        sp.wait_ge(s_wlo, n - 1)
                    sp.dma_start(w_raw[:, n % 2, :, :],
                                 w_v[half, :, 2 * q:2 * q + 2, :]).then_inc(s_wraw[n % 2], 16)
                load_w(0)
                load_w(1)
                sp.dma_start(xt[:, 1, :], x[P:2 * P, :]).then_inc(s_x[1], 16)
                load_w(2)
                load_w(3)
                with sp.Fori(1, NB // 2) as i:
                    for p in range(2):
                        sp.wait_ge(s_tr, 2 * i + p - 1)
                        sp.dma_start(xt[:, p, :], x[bass.ts(2 * i + p, P), :]).then_inc(s_x[p], 16)
                for n in range(QW, 2 * QW):
                    load_w(n)
                for p in range(2):
                    sp.wait_ge(s_wlo, 2 * QW - 1 + p)
                    sp.dma_start(raw[:, p, :], w_qkg[p].rearrange("p k n -> p (k n)")).then_inc(s_tile[p], 16)
                sp.wait_ge(s_zero, 1)
                sp.dma_start(v_dram[S, :].rearrange("(a n) -> a n", n=CH), zeros[:]).then_inc(s_zout, 16)
                sp.wait_ge(s_zout, 16)
                for p in range(2):
                    sp.wait_ge(s_vout[p], 16 * NB)

            @block.gpsimd
            def _(pool):
                nc.gpsimd.memset(ident[:], 0.0).then_inc(s_ident, 1)
                pool.wait_ge(s_ident, 1)
                nc.gpsimd.affine_select(out=ident[:], in_=ident[:], compare_op=ALU.not_equal, fill=1.0, base=0,
                                        pattern=[[-1, P]], channel_multiplier=1).then_inc(s_ident, 1)
                with pool.Fori(0, NB // 2) as i:
                    for p in range(2):
                        pool.wait_ge(s_lo, 4 * i + 2 * p + 2)
                        pass_waits(pool, s_passed)
                        nc.gpsimd.tensor_copy(hT_lo[:, :, bass.ts(2 * i + p, P)], as_f32(stg_lo[p][:])).then_inc(s_keep_lo, 1)

            @block.scalar
            def _(act):
                def squares(s, p, first=False):
                    act.wait_ge(s_x[p], 8 * (s - p) + 16)
                    if not first:
                        act.wait_ge(s_sumsq, s)
                    nc.scalar.activation(junk[:], xt[:, p, :], ACT.Square,
                                         accum_out=stat[:, p, 0:1]).then_inc(s_sumsq, 1)

                def root(s, p):
                    act.wait_ge(s_mean, s + 1)
                    nc.scalar.activation(stat[:, p, 2:3], stat[:, p, 1:2], ACT.Sqrt).then_inc(s_root, 1)

                def stage_hi(s, p, first):
                    act.wait_ge(s_tr, s + 1)
                    if not first:
                        act.wait_ge(s_v, s - 1)
                        act.wait_ge(s_keep_hi, s - 1)
                    for q in range(2):
                        nc.scalar.activation(stg_hi[p][:, 4 * q:4 * q + 4, :].rearrange("p k t -> p (k t)"),
                                             tp[p][q][:], ACT.Copy).then_inc(s_hi, 1)

                def evacuate(s, p, first):
                    act.wait_ge(s_v, s + 1)
                    if not first:
                        act.wait_ge(s_vout[p], 8 * (s - p))
                    nc.scalar.activation(vst[:, p, :], vp[p][:], ACT.Copy).then_inc(s_vst, 1)

                def store(s, p, rows, half):
                    act.wait_ge(s_vst, s + 1)
                    act.dma_start(v_dram[rows, half * CH:(half + 1) * CH], vst[:, p, :]).then_inc(s_vout[p], 16)

                def hi_w(n):
                    if n >= QW:
                        if n < 2 * QW - 1:
                            act.wait_ge(s_wused, n - QW + 1)
                        else:
                            act.wait_ge(s_v, NB)
                    act.wait_ge(s_wraw[n % 2], 16 * (n // 2 + 1))
                    nc.scalar.activation(w_hi[:, quarter[n % QW], :], w_raw[:, n % 2, :, :], ACT.Copy).then_inc(s_whi, 1)

                squares(0, 0, True)
                root(0, 0)
                hi_w(0)
                stage_hi(0, 0, True)
                for n in range(1, QW):
                    hi_w(n)
                squares(1, 1)
                root(1, 1)
                squares(2, 0)
                root(2, 0)
                stage_hi(1, 1, True)
                evacuate(0, 0, True)
                store(0, 0, slice(0, P), 0)
                squares(3, 1)
                root(3, 1)
                stage_hi(2, 0, False)
                evacuate(1, 1, True)
                store(1, 1, slice(P, 2 * P), 0)
                with act.Fori(1, NB // 2 - 1) as i:
                    squares(2 * i + 2, 0)
                    root(2 * i + 2, 0)
                    stage_hi(2 * i + 1, 1, False)
                    evacuate(2 * i, 0, False)
                    store(2 * i, 0, bass.ts(2 * i, P), 0)
                    squares(2 * i + 3, 1)
                    root(2 * i + 3, 1)
                    stage_hi(2 * i + 2, 0, False)
                    evacuate(2 * i + 1, 1, False)
                    store(2 * i + 1, 1, bass.ts(2 * i + 1, P), 0)
                stage_hi(NB - 1, 1, False)
                evacuate(NB - 2, 0, False)
                store(NB - 2, 0, slice((NB - 2) * P, (NB - 1) * P), 0)
                for n in range(QW, 2 * QW):
                    hi_w(n)
                evacuate(NB - 1, 1, False)
                store(NB - 1, 1, slice((NB - 1) * P, NB * P), 0)
                with act.Fori(0, NB // 2) as i:
                    for p in range(2):
                        evacuate(NB + 2 * i + p, p, False)
                        store(NB + 2 * i + p, p, bass.ts(2 * i + p, P), 1)

            @block.vector
            def _(dve):
                def mean(s, p):
                    dve.wait_ge(s_sumsq, s + 1)
                    nc.vector.tensor_scalar(stat[:, p, 1:2], stat[:, p, 0:1], 1.0 / D, EPS, ALU.mult, ALU.add).then_inc(s_mean, 1)

                def normed(s, p):
                    dve.wait_ge(s_root, s + 1)
                    rms_chain(nc, dve, s_chain, CHAIN * s, stat[:, p, 1:2], stat[:, p, 2:3], stat[:, p, 3:4], stat[:, p, 4:5])
                    nc.vector.scalar_tensor_tensor(xt[:, p, :], xt[:, p, :], stat[:, p, 3:4], norm_row[:],
                                                   ALU.mult, ALU.mult).then_inc(s_h, 1)

                def stage_lo(s, p, first):
                    if not first:
                        dve.wait_ge(s_keep_lo, s - 1)
                    for q in range(2):
                        dve.wait_ge(s_hi, 2 * s + q + 1)
                        nc.vector.tensor_tensor(stg_lo[p][:, 4 * q:4 * q + 4, :].rearrange("p k t -> p (k t)"), tp[p][q][:],
                                                as_f32(stg_hi[p][:, 4 * q:4 * q + 4, :].rearrange("p k t -> p (k t)")),
                                                ALU.subtract).then_inc(s_lo, 1)

                def keep_hi(s, p, cols):
                    nc.vector.tensor_copy(hT_hi[:, :, cols], as_f32(stg_hi[p][:])).then_inc(s_keep_hi, 1)

                def lo_w(n):
                    dve.wait_ge(s_whi, n + 1)
                    nc.vector.tensor_tensor(w_lo[:, quarter[n % QW], :], w_raw[:, n % 2, :, :],
                                            as_f32(w_hi[:, quarter[n % QW], :]), ALU.subtract).then_inc(s_wlo, 1)

                nc.vector.memset(zeros[:], 0.0).then_inc(s_zero, 1)
                dve.wait_ge(s_norm, 16)
                mean(0, 0)
                normed(0, 0)
                lo_w(0)
                stage_lo(0, 0, True)
                for n in range(1, QW):
                    lo_w(n)
                keep_hi(0, 0, slice(0, P))
                mean(1, 1)
                normed(1, 1)
                mean(2, 0)
                normed(2, 0)
                stage_lo(1, 1, True)
                keep_hi(1, 1, slice(P, 2 * P))
                with dve.Fori(1, NB // 2 - 1) as i:
                    mean(2 * i + 1, 1)
                    normed(2 * i + 1, 1)
                    stage_lo(2 * i, 0, False)
                    keep_hi(2 * i, 0, bass.ts(2 * i, P))
                    mean(2 * i + 2, 0)
                    normed(2 * i + 2, 0)
                    stage_lo(2 * i + 1, 1, False)
                    keep_hi(2 * i + 1, 1, bass.ts(2 * i + 1, P))
                mean(NB - 1, 1)
                normed(NB - 1, 1)
                for s in (NB - 2, NB - 1):
                    stage_lo(s, s % 2, False)
                    keep_hi(s, s % 2, slice(s * P, (s + 1) * P))
                def reload(s, p, cols):
                    dve.wait_ge(s_v, s - 1)
                    nc.vector.tensor_copy(stg_hi[p][:], as_f32(hT_hi[:, :, cols]))
                    nc.vector.tensor_copy(stg_lo[p][:], as_f32(hT_lo[:, :, cols])).then_inc(s_stage, 1)

                dve.wait_ge(s_keep_hi, NB)
                dve.wait_ge(s_keep_lo, NB)
                reload(NB, 0, slice(0, P))
                for n in range(QW, 2 * QW):
                    lo_w(n)
                reload(NB + 1, 1, slice(P, 2 * P))
                with dve.Fori(1, NB // 2) as i:
                    for p in range(2):
                        reload(NB + 2 * i + p, p, bass.ts(2 * i + p, P))

            @block.tensor
            def _(pe):
                def transposes(s, p):
                    pe.wait_ge(s_h, s + 1)
                    for k in range(KT):
                        last = nc.tensor.transpose(tp[p][k // 4][:, (k % 4) * P:(k % 4 + 1) * P],
                                                   xt[:, p, k * P:(k + 1) * P], ident[:])
                    last.then_inc(s_tr, 1)

                def project(s, p, first, staged, count, halves=None, leaves=False):
                    pe.wait_ge(staged, count)
                    if not first:
                        pe.wait_ge(s_vst, s - 1)
                    for k in range(KT):
                        if halves is not None and k % 2 == 0:
                            pe.wait_ge(s_wlo, halves * QW + k // 2 + 1)
                        for n, (a, b) in enumerate(((stg_hi, w_hi), (stg_hi, w_lo), (stg_lo, w_hi))):
                            last = nc.tensor.matmul(vp[p][:], a[p][:, k, :], b[:, k, :],
                                                    start=(k == 0 and n == 0), stop=(k == KT - 1 and n == 2))
                        if leaves and k % 2 == 1 and k < KT - 1:
                            last.then_inc(s_wused, 1)
                    last.then_inc(s_v, 1)

                pe.wait_ge(s_ident, 2)
                transposes(0, 0)
                project(0, 0, True, s_lo, 2, halves=0)
                transposes(1, 1)
                transposes(2, 0)
                project(1, 1, True, s_lo, 4)
                with pe.Fori(1, NB // 2 - 1) as i:
                    transposes(2 * i + 1, 1)
                    project(2 * i, 0, False, s_lo, 4 * i + 2)
                    transposes(2 * i + 2, 0)
                    project(2 * i + 1, 1, False, s_lo, 4 * i + 4)
                transposes(NB - 1, 1)
                project(NB - 2, 0, False, s_lo, 2 * NB - 2)
                project(NB - 1, 1, False, s_lo, 2 * NB, leaves=True)
                project(NB, 0, False, s_stage, 1, halves=1)
                project(NB + 1, 1, False, s_stage, 2)
                with pe.Fori(1, NB // 2) as i:
                    for p in range(2):
                        project(NB + 2 * i + p, p, False, s_stage, 2 * i + p + 1)


def phase_qkg(nc, w_qkg, v_dram, qk_hi, qk_lo, g_dram, dv_dram, vb_dram, hT_hi, hT_lo, raw, s_wraw):
    with ExitStack() as ctx:
        def sb(name, shape, dt):
            return ctx.enter_context(nc.sbuf_tensor(name, shape, dt))

        def sem(name):
            return ctx.enter_context(nc.semaphore(name))

        w_raw = raw[:].rearrange("p a (k n) -> p a k n", k=KT)
        w_hi = [sb(f"w_hi{p}", [P, KT, P], F32R) for p in range(2)]
        w_lo = [sb(f"w_lo{p}", [P, KT, P], F32R) for p in range(2)]
        out_hi = [sb(f"out_hi{p}", [P, NC, CH], F32) for p in range(2)]
        out_lo = [sb(f"out_lo{p}", [P, NC, CH], F32) for p in range(2)]
        va = sb("v_here", [P, D], F32)
        vb = sb("v_next", [P, D], F32)
        dv = sb("dv_parts", [P, H, 2, DH], F32R)
        pp = [[ctx.enter_context(nc.psum_tensor(f"proj_ps{p}{c}", [P, CH], F32)) for c in range(NC)] for p in range(2)]

        s_whi0 = sem("first_w_hi_ready")
        s_wlo0 = sem("first_w_lo_ready")
        s_whi = sem("w_hi_ready")
        s_wlo = sem("w_lo_ready")
        s_pp = sem("projection_ready")
        s_ohi = sem("out_hi_ready")
        s_olo = sem("out_lo_ready")
        s_out = [sem(f"tile_stored{p}") for p in range(2)]
        s_passed = sem("waits_passed_qkg")
        s_va = sem("v_loaded")
        s_dif = sem("dv_ready")
        s_dhi = sem("dv_hi_ready")
        s_dlo = sem("dv_lo_ready")
        s_dout = sem("dv_stored")

        NT = 3 * KT
        NQK = 2 * KT

        with nc.Block() as block:
            @block.sync
            def _(sp):
                sp.dma_start(va[0:NB, :], v_dram[0:S, :].rearrange("(b p) n -> b p n", p=P)[:, 0, :]).then_inc(s_va, 16)
                sp.wait_ge(s_dlo, 1)
                sp.dma_start(vb_dram[:], as_f32(dv[0:NB]).rearrange("b h a n -> b (h a n)")).then_inc(s_dout, 16)
                sp.dma_start(va[:], v_dram[0:P, :]).then_inc(s_va, 16)
                sp.dma_start(vb[:], v_dram[1:P + 1, :]).then_inc(s_va, 16)

                def load_dv(t):
                    sp.dma_start(va[:], v_dram[bass.ds(t * P, P), :]).then_inc(s_va, 16)
                    sp.dma_start(vb[:], v_dram[bass.ds(t * P + 1, P), :]).then_inc(s_va, 16)

                def store_dv(t):
                    sp.wait_ge(s_dlo, t + 2)
                    pass_waits(sp, s_passed)
                    sp.dma_start(dv_dram[:, :, t, :].rearrange("h p n -> p h n"),
                                 as_f32(dv[:]).rearrange("p h a n -> p h (a n)")).then_inc(s_dout, 16)

                def load(t, p, first=False):
                    if first:
                        sp.wait_ge(s_wlo0, t + 1)
                    else:
                        sp.wait_ge(s_wlo, t - 1)
                    sp.dma_start(w_raw[:, p, :, :], w_qkg[t + 2]).then_inc(s_wraw[p], 16)

                def store(t, p):
                    rows = bass.ds(t * P, P)
                    sp.wait_ge(s_olo, NC * (t + 1))
                    sp.dma_start(qk_hi[rows, :], out_hi[p][:].rearrange("p c n -> p (c n)")).then_inc(s_out[p], 16)
                    sp.dma_start(qk_lo[rows, :], out_lo[p][:].rearrange("p c n -> p (c n)")).then_inc(s_out[p], 16)

                def store_gate(t, p):
                    sp.wait_ge(s_olo, NC * (t + 1))
                    sp.dma_start(g_dram[bass.ds((t - NQK) * P, P), :],
                                 out_lo[p][:].rearrange("p c n -> p (c n)")).then_inc(s_out[p], 16)

                for p in range(2):
                    load(p, p, True)
                    store_dv(p)
                    load_dv(p + 1)
                    store(p, p)
                with sp.Fori(1, NQK // 2 - 1) as i:
                    for p in range(2):
                        load(2 * i + p, p)
                        store_dv(2 * i + p)
                        load_dv(2 * i + p + 1)
                        store(2 * i + p, p)
                for p in range(2):
                    load(NQK - 2 + p, p)
                    store_dv(NQK - 2 + p)
                    if p == 0:
                        load_dv(NQK - 1)
                    store(NQK - 2 + p, p)
                with sp.Fori(NQK // 2, NT // 2 - 1) as i:
                    for p in range(2):
                        load(2 * i + p, p)
                        store_gate(2 * i + p, p)
                for p in range(2):
                    store_gate(NT - 2 + p, p)
                for p in range(2):
                    sp.wait_ge(s_out[p], 16 * NQK + 8 * (NT - NQK))
                sp.wait_ge(s_dout, 16 * (NB + 1))

            @block.gpsimd
            def _(pool):
                def split(t, p):
                    pool.wait_ge(s_wraw[p], 8 * (t - p) + 16)
                    pool.wait_ge(s_pp, NC * (t - 1))
                    pass_waits(pool, s_passed)
                    nc.gpsimd.tensor_copy(w_hi[p][:], w_raw[:, p, :, :]).then_inc(s_whi, 1)
                    pool.wait_ge(s_whi, t - 1)
                    nc.gpsimd.tensor_tensor(w_lo[p][:], w_raw[:, p, :, :], as_f32(w_hi[p][:]), ALU.subtract).then_inc(s_wlo, 1)
                with pool.Fori(1, NT // 2) as i:
                    for p in range(2):
                        split(2 * i + p, p)

            @block.tensor
            def _(pe):
                def tile(t, p, first):
                    pe.wait_ge(s_wlo0 if first else s_wlo, t + 1 if first else t - 1)
                    for c in range(NC):
                        if not first:
                            pe.wait_ge(s_olo, NC * (t - 2) + c + 1)
                        cols = slice(c * CH, (c + 1) * CH)
                        for k in range(KT):
                            for n, (a, b) in enumerate(((w_hi, hT_hi), (w_hi, hT_lo), (w_lo, hT_hi))):
                                last = nc.tensor.matmul(pp[p][c][:], a[p][:, k, :], b[:, k, cols],
                                                        start=(k == 0 and n == 0), stop=(k == KT - 1 and n == 2))
                        last.then_inc(s_pp, 1)
                for p in range(2):
                    tile(p, p, True)
                with pe.Fori(1, NT // 2) as i:
                    for p in range(2):
                        tile(2 * i + p, p, False)

            @block.scalar
            def _(act):
                def dv_hi(t, rows=P):
                    nc.scalar.activation(dv[0:rows, :, 0, :], va[0:rows, :].rearrange("p (h n) -> p h n", h=H),
                                         ACT.Copy).then_inc(s_dhi, 1)

                def tile_hi(t, p, first, func, stores):
                    def out(c):
                        return out_hi[p][:, c, :].bitcast(F32R) if func == ACT.Copy else out_hi[p][:, c, :]
                    if not first:
                        act.wait_ge(s_out[p], stores)
                    for c in range(NC):
                        act.wait_ge(s_pp, NC * t + c + 1)
                        nc.scalar.activation(out(c), pp[p][c][:], func).then_inc(s_ohi, 1)
                def dv_hi_of(t):
                    act.wait_ge(s_dif, t + 1)
                    act.wait_ge(s_dout, 16 * (t + 1))
                    dv_hi(t)

                for p in range(2):
                    act.wait_ge(s_wraw[p], 16)
                    nc.scalar.activation(w_hi[p][:], w_raw[:, p, :, :], ACT.Copy).then_inc(s_whi0, 1)
                act.wait_ge(s_va, 16)
                dv_hi(-1, NB)
                for p in range(2):
                    dv_hi_of(p)
                    tile_hi(p, p, True, ACT.Copy, None)
                with act.Fori(1, NQK // 2) as i:
                    for p in range(2):
                        dv_hi_of(2 * i + p)
                        tile_hi(2 * i + p, p, False, ACT.Copy, 32 * i)
                with act.Fori(NQK // 2, NT // 2) as i:
                    for p in range(2):
                        tile_hi(2 * i + p, p, False, ACT.Sigmoid, 16 * i + 16 * NQK // 2)

            @block.vector
            def _(dve):
                def dv_lo(t, rows=P):
                    dve.wait_ge(s_dhi, t + 2)
                    nc.vector.tensor_tensor(dv[0:rows, :, 1, :], va[0:rows, :].rearrange("p (h n) -> p h n", h=H),
                                            as_f32(dv[0:rows, :, 0, :]), ALU.subtract).then_inc(s_dlo, 1)

                def dif(t):
                    dve.wait_ge(s_va, 32 * (t + 1) + 16)
                    nc.vector.tensor_tensor(va[:], vb[:], va[:], ALU.subtract).then_inc(s_dif, 1)

                def tile_lo(t, p, op, stores, first):
                    if not first:
                        dve.wait_ge(s_out[p], stores)
                    for c in range(NC):
                        dve.wait_ge(s_ohi, NC * t + c + 1)
                        nc.vector.tensor_tensor(out_lo[p][:, c, :], pp[p][c][:], out_hi[p][:, c, :], op).then_inc(s_olo, 1)
                for p in range(2):
                    dve.wait_ge(s_whi0, p + 1)
                    nc.vector.tensor_tensor(w_lo[p][:], w_raw[:, p, :, :], as_f32(w_hi[p][:]), ALU.subtract).then_inc(s_wlo0, 1)
                dv_lo(-1, NB)
                for p in range(2):
                    dif(p)
                    dv_lo(p)
                    tile_lo(p, p, ALU.subtract, None, True)
                with dve.Fori(1, NQK // 2) as i:
                    for p in range(2):
                        dif(2 * i + p)
                        dv_lo(2 * i + p)
                        tile_lo(2 * i + p, p, ALU.subtract, 32 * i, False)
                with dve.Fori(NQK // 2, NT // 2) as i:
                    for p in range(2):
                        tile_lo(2 * i + p, p, ALU.mult, 16 * i + 16 * NQK // 2, False)


def head_steps():
    return [(c, j, r) for c in range(NC) for j in range(c, NC) for r in range(CB)]


STEPS = head_steps()
HS = len(STEPS)
PAIR = 2 * HS
LEAD_SCORES = 8
LEAD_SCAN = 6
LEAD_TURN = 3
RU, RZ, RT, RO = 4, 2, 4, 2


def phase_attention(nc, qk_hi, qk_lo, dv_dram, vb_dram, w_out, o_hi, o_lo, wo_hi, wo_lo, ident):
    with ExitStack() as ctx:
        def sb(name, shape, dt):
            return ctx.enter_context(nc.sbuf_tensor(name, shape, dt))

        def pb(name):
            return ctx.enter_context(nc.psum_tensor(name, [P, CH], F32))

        def sem(name):
            return ctx.enter_context(nc.semaphore(name))

        q_t = [sb(f"q_parts{p}", [P, S], F32R) for p in range(2)]
        kh_t = [sb(f"k_hi_twice{p}", [P, S], F32R) for p in range(2)]
        kl_t = [sb(f"k_lo_twice{p}", [P, S], F32R) for p in range(2)]
        dv_t = [sb(f"dv_head{p}", [P, NB, P], F32R) for p in range(2)]
        vb_t = [sb(f"v_first{p}", [NB, P], F32R) for p in range(2)]
        block_of = sb("block_of_token", [NB, S], F32R)
        u_t = [[sb(f"u{n}_{r}", [P, CH], F32) for r in range(CB)] for n in range(RU)]
        rt_hi = [sb(f"r_turned_hi{n}", [P, CH], F32R) for n in range(RT)]
        rt_lo = [sb(f"r_turned_lo{n}", [P, CH], F32R) for n in range(RT)]
        o_st = [sb(f"o_stage{n}", [P, CH], F32) for n in range(RO)]
        wo_raw = sb("w_out_raw", [P, D], F32)
        unbroken = sb("unbroken", [P, CH], F32)
        z_ps = [pb(f"z_ps{n}") for n in range(RZ)]
        t_ps = [pb(f"turn_ps{n}") for n in range(RT)]
        o_ps = [pb(f"o_ps{n}") for n in range(RO)]

        s_qk = [sem(f"qk_loaded{p}") for p in range(2)]
        s_chunk = [sem(f"first_chunk_loaded{j}") for j in range(NC)]
        s_dv = [sem(f"dv_loaded{p}") for p in range(2)]
        s_const = sem("constants_ready")
        s_z = sem("scores_ready")
        s_u = sem("u_ready")
        s_r = sem("scan_ready")
        s_t = sem("turned")
        s_hi = sem("r_hi_ready")
        s_lo = sem("r_lo_ready")
        s_o = sem("o_ready")
        s_ost = sem("o_evacuated")
        s_oout = [sem(f"o_stored{n}") for n in range(2)]
        s_passed = sem("waits_passed_attention")
        s_woraw = sem("w_out_raw_loaded")
        s_wohi = sem("w_out_hi_ready")
        s_wolo = sem("w_out_lo_ready")

        NLOAD = 6 * 16

        def score_cols(m):
            c, j, r = STEPS[m % HS]
            return r * P if j == c else 0

        def turn_width(m):
            c, j, r = STEPS[m % HS]
            return (r + 1) * P if j == c else CH

        with nc.Block() as block:
            @block.sync
            def _(sp):
                def load(h, p):
                    rows = bass.ds(h * DH, DH)
                    krows = bass.ds(h * DH + D, DH)
                    for half in range(2):
                        part = slice(half * DH, (half + 1) * DH)
                        sp.dma_start(as_f32(q_t[p][part, :]), (qk_hi, qk_lo)[half][rows, :]).then_inc(s_qk[p], 16)
                        sp.dma_start(as_f32(kh_t[p][part, :]), qk_hi[krows, :]).then_inc(s_qk[p], 16)
                        sp.dma_start(as_f32(kl_t[p][part, :]), qk_lo[krows, :]).then_inc(s_qk[p], 16)

                def load_v(h, p):
                    sp.dma_start(as_f32(dv_t[p][:]), dv_dram[h]).then_inc(s_dv[p], 16)
                    sp.dma_start(as_f32(vb_t[p][:]), vb_dram[:, bass.ds(h * P, P)]).then_inc(s_dv[p], 16)
                def load_chunk(j):
                    cols = slice(j * CH, (j + 1) * CH)
                    for half, src in enumerate((qk_hi, qk_lo)):
                        sp.dma_start(as_f32(q_t[0][half * DH:(half + 1) * DH, cols]), src[0:DH, cols]).then_inc(s_chunk[j], 16)
                        for half2 in range(2):
                            sp.dma_start(as_f32((kh_t, kl_t)[half][0][half2 * DH:(half2 + 1) * DH, cols]),
                                         src[D:D + DH, cols]).then_inc(s_chunk[j], 16)

                for j in range(NC):
                    load_chunk(j)
                load_v(0, 0)
                load(1, 1)
                load_v(1, 1)

                def store(pairs, g):
                    c, p = g % NC, g // NC
                    sp.wait_ge(s_ost, NC * 2 * pairs + g + 1)
                    pass_waits(sp, s_passed)
                    rows = bass.ds((2 * pairs + p) * DH, DH)
                    sp.dma_start(o_hi[rows, c * CH:(c + 1) * CH], o_st[c % RO][0:DH, :]).then_inc(s_oout[c % RO], 16)
                    sp.dma_start(o_lo[rows, c * CH:(c + 1) * CH], o_st[c % RO][DH:P, :]).then_inc(s_oout[c % RO], 16)

                with sp.Fori(0, H // 2 - 1) as i:
                    for p in range(2):
                        for c in range(NC):
                            store(i, NC * p + c)
                        load(2 * i + 2 + p, p)
                        load_v(2 * i + 2 + p, p)
                for g in range(2 * NC):
                    store(H // 2 - 1, g)
                for n in range(2):
                    sp.wait_ge(s_oout[n], 32 * H * NC // 2)

            @block.gpsimd
            def _(pool):
                tmp = as_f32(block_of[:])
                nc.gpsimd.memset(unbroken[:], 1.0).then_inc(s_const, 1)
                nc.gpsimd.memset(tmp, 1.0).then_inc(s_const, 1)
                pool.wait_ge(s_const, 2)
                nc.gpsimd.affine_select(out=unbroken[:], in_=unbroken[:], compare_op=ALU.is_ge, fill=0.0, base=0,
                                        pattern=[[-1, CH]], channel_multiplier=1).then_inc(s_const, 1)
                nc.gpsimd.affine_select(out=block_of[:], in_=tmp, compare_op=ALU.is_ge, fill=0.0, base=0,
                                        pattern=[[1, S]], channel_multiplier=-P).then_inc(s_const, 1)
                pool.wait_ge(s_const, 4)
                nc.gpsimd.affine_select(out=block_of[:], in_=tmp, compare_op=ALU.is_ge, fill=0.0, base=P - 1,
                                        pattern=[[-1, S]], channel_multiplier=P).then_inc(s_const, 1)
                for k in range(KT):
                    if k:
                        pool.wait_ge(s_wolo, k)
                    pool.dma_start(wo_raw[:], w_out[k * P:(k + 1) * P, :]).then_inc(s_woraw, 16)
                    pool.wait_ge(s_woraw, 16 * (k + 1))
                    nc.gpsimd.tensor_copy(wo_hi[:, k, :], wo_raw[:]).then_inc(s_wohi, 1)
                    pool.wait_ge(s_wohi, k + 1)
                    nc.gpsimd.tensor_tensor(wo_lo[:, k, :], wo_raw[:], as_f32(wo_hi[:, k, :]), ALU.subtract).then_inc(s_wolo, 1)


            def over_pairs(eng, body):
                body(0, True, False)
                with eng.Fori(1, H // 2 - 1) as i:
                    body(i * PAIR, False, False)
                body((H // 2 - 1) * PAIR, False, True)

            @block.tensor
            def _(pe):
                def scores(at, m):
                    p, (c, j, r) = (m // HS) % 2, STEPS[m % HS]
                    lo = score_cols(m)
                    tau = slice(c * CH + r * P, c * CH + (r + 1) * P)
                    sig = slice(j * CH + lo, (j + 1) * CH)
                    out = z_ps[m % RZ][:, 0:CH - lo]
                    nc.tensor.matmul(out, q_t[p][:, tau], kh_t[p][:, sig], start=True, stop=False)
                    nc.tensor.matmul(out, q_t[p][:, tau], kl_t[p][:, sig], start=False, stop=True).then_inc(s_z, 1)

                def scores_waits(at, m, first):
                    p = (m // HS) % 2
                    if first and m < NC * CB:
                        if m % CB == 0:
                            pe.wait_ge(s_chunk[m // CB], NLOAD)
                    elif m % HS == 0:
                        pe.wait_ge(s_qk[p], NLOAD * (at // PAIR + m // PAIR + p))
                    pe.wait_ge(s_u, at + m - RZ + 1)

                def turn(m):
                    c, j, r = STEPS[m % HS]
                    unit = (m // CB) % RU
                    for t in range(turn_width(m) // P):
                        lo = t * P if j == c else 0
                        last = nc.tensor.transpose(t_ps[m % RT][:, t * P:(t + 1) * P],
                                                   u_t[unit][t][:, r * P - lo:(r + 1) * P - lo], ident[:])
                    last.then_inc(s_t, 1)

                def scans_for(m):
                    c, j, r = STEPS[m % HS]
                    return m + 1 if j == c else m - r + CB

                def weigh(m):
                    p, (c, j, r) = (m // HS) % 2, STEPS[m % HS]
                    w = turn_width(m)
                    out = o_ps[c % RO]
                    if j == c and r == 0:
                        nc.tensor.matmul(out[:], vb_t[p][:], block_of[:, c * CH:(c + 1) * CH], start=True, stop=False)
                    end = j == NC - 1 and r == CB - 1
                    weights = dv_t[p][:, j * CB + r, :]
                    nc.tensor.matmul(out[:, 0:w], weights, rt_hi[m % RT][:, 0:w], start=False, stop=False)
                    last = nc.tensor.matmul(out[:, 0:w], weights, rt_lo[m % RT][:, 0:w], start=False, stop=end)
                    if end:
                        last.then_inc(s_o, 1)

                pe.wait_ge(s_const, 5)
                for m in range(LEAD_SCORES):
                    if m % CB == 0:
                        pe.wait_ge(s_chunk[m // CB], NLOAD)
                    if m >= RZ:
                        pe.wait_ge(s_u, m - RZ + 1)
                    scores(0, m)
                for m in range(LEAD_TURN):
                    pe.wait_ge(s_r, scans_for(m))
                    turn(m)

                def pair(at, first, last):
                    for n in range(PAIR):
                        if n % HS == 0:
                            pe.wait_ge(s_dv[n // HS], 32 * (at // PAIR + 1))
                        if n + LEAD_SCORES < PAIR or not last:
                            scores_waits(at, n + LEAD_SCORES, first)
                            scores(at, n + LEAD_SCORES)
                        if n + LEAD_TURN < PAIR or not last:
                            pe.wait_ge(s_r, at + scans_for(n + LEAD_TURN))
                            turn(n + LEAD_TURN)
                        pe.wait_ge(s_lo, at + n + 1)
                        weigh(n)
                over_pairs(pe, pair)

            @block.scalar
            def _(act):
                def stick(at, m):
                    w = CH - score_cols(m)
                    act.wait_ge(s_z, at + m + 1)
                    nc.scalar.activation(u_t[(m // CB) % RU][STEPS[m % HS][2]][:, 0:w], z_ps[m % RZ][:, 0:w],
                                         ACT.Sigmoid, scale=-Z_SCALE).then_inc(s_u, 1)

                def hi(at, m):
                    w = turn_width(m)
                    act.wait_ge(s_t, at + m + 1)
                    nc.scalar.activation(rt_hi[m % RT][:, 0:w], t_ps[m % RT][:, 0:w], ACT.Copy).then_inc(s_hi, 1)

                def chunk_end(m):
                    c, j, r = STEPS[m % HS]
                    return NC * (m // HS) + c if j == NC - 1 and r == CB - 1 else None

                def empty(at, g, first):
                    c, pairs = g % NC, at // PAIR
                    act.wait_ge(s_o, NC * 2 * pairs + g + 1)
                    if not (first and g < RO):
                        act.wait_ge(s_oout[c % RO], 32 * (NC * pairs + g // RO))
                    nc.scalar.activation(o_st[c % RO][:], o_ps[c % RO][:], ACT.Copy).then_inc(s_ost, 1)

                for m in range(LEAD_SCAN):
                    stick(0, m)
                for m in range(LEAD_TURN):
                    stick(0, m + LEAD_SCAN)
                    hi(0, m)

                def pair(at, first, last):
                    for m in range(LEAD_TURN, PAIR + LEAD_TURN):
                        if m + LEAD_SCAN < PAIR or not last:
                            stick(at, m + LEAD_SCAN)
                        done = chunk_end(m - LEAD_TURN)
                        if done is not None:
                            empty(at, done, first)
                        if m < PAIR or not last:
                            hi(at, m)
                over_pairs(act, pair)

            @block.vector
            def _(dve):
                def scan(at, m):
                    c, j, r = STEPS[m % HS]
                    u = u_t[(m // CB) % RU][r][:, 0:CH - score_cols(m)]
                    start, other, op = 1.0, unbroken[:, 0:CH - score_cols(m)], ALU.max
                    if j != c:
                        other, op = u, ALU.min
                        w = CH - score_cols(m - CB)
                        start = u_t[(m // CB - 1) % RU][r][:, w - 1:w]
                        dve.wait_ge(s_r, at + m - CB + 1)
                    dve.wait_ge(s_u, at + m + 1)
                    nc.vector.tensor_tensor_scan(u, u, other, start, ALU.mult, op).then_inc(s_r, 1)

                def lo(at, m):
                    w = turn_width(m)
                    dve.wait_ge(s_hi, at + m + 1)
                    nc.vector.tensor_tensor(rt_lo[m % RT][:, 0:w], t_ps[m % RT][:, 0:w],
                                            as_f32(rt_hi[m % RT][:, 0:w]), ALU.subtract).then_inc(s_lo, 1)

                dve.wait_ge(s_const, 5)
                for m in range(LEAD_SCAN):
                    scan(0, m)

                def pair(at, first, last):
                    for m in range(PAIR):
                        if m + LEAD_SCAN < PAIR or not last:
                            scan(at, m + LEAD_SCAN)
                        lo(at, m)
                over_pairs(dve, pair)


def phase_output(nc, x, final_norm, o_hi, o_lo, g_dram, out, wo_hi, wo_lo):
    with ExitStack() as ctx:
        def sb(name, shape, dt):
            return ctx.enter_context(nc.sbuf_tensor(name, shape, dt))

        def sem(name):
            return ctx.enter_context(nc.semaphore(name))

        GB = 2
        GT = GB * P
        NG = S // GT
        oa = sb("o_part_hi", [P, 2, KT, GT], F32)
        ob = sb("o_part_lo", [P, 2, KT, GT], F32)
        gt = sb("gate", [P, 2, KT, GT], F32)
        m_hi = [sb(f"gated_hi{p}", [P, KT, GT], F32R) for p in range(2)]
        m_lo = [sb(f"gated_lo{p}", [P, KT, GT], F32R) for p in range(2)]
        xt = sb("x_again", [P, GB, D], F32)
        norm_row = sb("final_norm_row", [P, D], F32)
        junk = sb("square_junk2", [P, D], BF16)
        stat = sb("stat2", [P, GB, 5], F32)
        yp = [[[ctx.enter_context(nc.psum_tensor(f"y_ps{p}{b}{f}", [P, CH], F32)) for f in range(2)]
               for b in range(GB)] for p in range(2)]

        s_norm = sem("final_norm_loaded")
        s_in = [sem(f"group_loaded{p}") for p in range(2)]
        s_x = [sem(f"x_again_loaded{b}") for b in range(GB)]
        s_sum = sem("o_parts_added")
        s_gated = sem("gated")
        s_mhi = sem("gated_hi_ready")
        s_mlo = sem("gated_lo_ready")
        s_y = sem("y_ready")
        s_res = sem("residual_added")
        s_sumsq = sem("y_sum_squares")
        s_mean = sem("y_mean_square")
        s_root = sem("y_root")
        s_chain = sem("y_rms_chain")
        s_out = sem("out_ready")
        s_stored = [sem(f"out_stored{b}") for b in range(GB)]

        with nc.Block() as block:
            @block.sync
            def _(sp):
                sp.dma_start(norm_row[:], final_norm.rearrange("(a n) -> a n", a=1).to_broadcast([P, D])).then_inc(s_norm, 16)

                def load(t, p):
                    for tile, src in ((oa, o_hi), (ob, o_lo), (gt, g_dram)):
                        sp.dma_start(tile[:, p, :, :],
                                     src.rearrange("(k p) t -> p k t", p=P)[:, :, bass.ds(t * GT, GT)]).then_inc(s_in[p], 16)

                def load_x(t, b, first):
                    if not first:
                        sp.wait_ge(s_stored[b], 16 * t)
                    sp.dma_start(xt[:, b, :], x[bass.ds(t * GT + b * P, P), :]).then_inc(s_x[b], 16)
                for p in range(2):
                    load(p, p)
                for b in range(GB):
                    load_x(0, b, True)
                with sp.Fori(0, NG // 2 - 1) as i:
                    for p in range(2):
                        t = 2 * i + p
                        sp.wait_ge(s_mlo, t + 1)
                        load(t + 2, p)
                        for b in range(GB):
                            load_x(t + 1, b, False)
                for b in range(GB):
                    load_x(NG - 1, b, False)
                for b in range(GB):
                    sp.wait_ge(s_stored[b], 16 * NG)

            @block.tensor
            def _(pe):
                def group(t, p, first):
                    pe.wait_ge(s_mlo, t + 1)
                    for b in range(GB):
                        if not first:
                            pe.wait_ge(s_res, GB * (t - 2) + b + 1)
                        tok = slice(b * P, (b + 1) * P)
                        for f in range(2):
                            cols = slice(f * CH, (f + 1) * CH)
                            for k in range(KT):
                                for n, (a, w) in enumerate(((m_hi, wo_hi), (m_hi, wo_lo), (m_lo, wo_hi))):
                                    last = nc.tensor.matmul(yp[p][b][f][:], a[p][:, k, tok], w[:, k, cols],
                                                            start=(k == 0 and n == 0), stop=(k == KT - 1 and n == 2))
                        last.then_inc(s_y, 1)
                for p in range(2):
                    group(p, p, True)
                with pe.Fori(1, NG // 2) as i:
                    for p in range(2):
                        group(2 * i + p, p, False)

            @block.vector
            def _(dve):
                def gate(t, p, first):
                    dve.wait_ge(s_in[p], 24 * (t - p) + 48)
                    nc.vector.tensor_tensor(oa[:, p], oa[:, p], ob[:, p], ALU.add).then_inc(s_sum, 1)
                    dve.wait_ge(s_sum, t + 1)
                    nc.vector.tensor_tensor(oa[:, p], oa[:, p], gt[:, p], ALU.mult).then_inc(s_gated, 1)
                    dve.wait_ge(s_mhi, t + 1)
                    nc.vector.tensor_tensor(m_lo[p][:], oa[:, p], as_f32(m_hi[p][:]), ALU.subtract).then_inc(s_mlo, 1)

                def finish(t, p, b):
                    n = GB * t + b
                    dve.wait_ge(s_y, n + 1)
                    dve.wait_ge(s_x[b], 16 * (t + 1))
                    for f in range(2):
                        cols = slice(f * CH, (f + 1) * CH)
                        last = nc.vector.tensor_tensor(xt[:, b, cols], yp[p][b][f][:], xt[:, b, cols], ALU.add)
                    last.then_inc(s_res, 1)
                    dve.wait_ge(s_sumsq, n + 1)
                    nc.vector.tensor_scalar(stat[:, b, 1:2], stat[:, b, 0:1], 1.0 / D, EPS, ALU.mult, ALU.add).then_inc(s_mean, 1)
                    dve.wait_ge(s_root, n + 1)
                    rms_chain(nc, dve, s_chain, CHAIN * n, stat[:, b, 1:2], stat[:, b, 2:3], stat[:, b, 3:4], stat[:, b, 4:5])
                    nc.vector.scalar_tensor_tensor(xt[:, b, :], xt[:, b, :], stat[:, b, 3:4], norm_row[:],
                                                   ALU.mult, ALU.mult).then_inc(s_out, 1)

                dve.wait_ge(s_norm, 16)
                gate(0, 0, True)
                gate(1, 1, True)
                for b in range(GB):
                    finish(0, 0, b)
                with dve.Fori(0, NG // 2 - 1) as i:
                    gate(2 * i + 2, 0, False)
                    for b in range(GB):
                        finish(2 * i + 1, 1, b)
                    gate(2 * i + 3, 1, False)
                    for b in range(GB):
                        finish(2 * i + 2, 0, b)
                for b in range(GB):
                    finish(NG - 1, 1, b)

            @block.scalar
            def _(act):
                def hi(t, p):
                    act.wait_ge(s_gated, t + 1)
                    nc.scalar.activation(m_hi[p][:], oa[:, p], ACT.Copy).then_inc(s_mhi, 1)

                def finish(t, b, first=False):
                    n = GB * t + b
                    act.wait_ge(s_res, n + 1)
                    if not first:
                        act.wait_ge(s_sumsq, n)
                    nc.scalar.activation(junk[:], xt[:, b, :], ACT.Square, accum_out=stat[:, b, 0:1]).then_inc(s_sumsq, 1)
                    act.wait_ge(s_mean, n + 1)
                    nc.scalar.activation(stat[:, b, 2:3], stat[:, b, 1:2], ACT.Sqrt).then_inc(s_root, 1)
                    act.wait_ge(s_out, n + 1)
                    act.dma_start(out[bass.ds(t * GT + b * P, P), :], xt[:, b, :]).then_inc(s_stored[b], 16)

                hi(0, 0)
                hi(1, 1)
                for b in range(GB):
                    finish(0, b, first=(b == 0))
                with act.Fori(0, NG // 2 - 1) as i:
                    act.wait_ge(s_y, 2 * GB * i + GB)
                    hi(2 * i + 2, 0)
                    for b in range(GB):
                        finish(2 * i + 1, b)
                    hi(2 * i + 3, 1)
                    for b in range(GB):
                        finish(2 * i + 2, b)
                for b in range(GB):
                    finish(NG - 1, b)


def stick_breaking_layer(nc, x, a_norm, w_v, w_qkg, w_out, final_norm, out):
    def scratch(name, shape, dt):
        return nc.dram_tensor(name, shape, dt, kind="Internal").ap()

    v_dram = scratch("v_rows", [S + 1, D], F32)
    qk_hi = scratch("qk_hi_cols", [2 * D, S], F32)
    qk_lo = scratch("qk_lo_cols", [2 * D, S], F32)
    g_dram = scratch("gate_cols", [D, S], F32)
    dv_dram = scratch("dv_parts_dram", [H, P, NB, P], F32)
    vb_dram = scratch("v_first_dram", [NB, H * P], F32)
    o_hi = scratch("o_hi_cols", [D, S], F32)
    o_lo = scratch("o_lo_cols", [D, S], F32)

    with ExitStack() as ctx:
        ident = ctx.enter_context(nc.sbuf_tensor("ident", [P, P], F32))
        with ExitStack() as projections:
            hT_hi = projections.enter_context(nc.sbuf_tensor("hT_hi", [P, KT, S], F32R))
            hT_lo = projections.enter_context(nc.sbuf_tensor("hT_lo", [P, KT, S], F32R))
            raw = projections.enter_context(nc.sbuf_tensor("w_raw", [P, 2, D], F32))
            s_tile = [projections.enter_context(nc.semaphore(f"w_tile_loaded{p}")) for p in range(2)]
            phase_norm_and_v(nc, x, a_norm, w_v, w_qkg, v_dram, hT_hi, hT_lo, ident, raw, s_tile)
            phase_qkg(nc, w_qkg, v_dram, qk_hi, qk_lo, g_dram, dv_dram, vb_dram, hT_hi, hT_lo, raw, s_tile)
        wo_hi = ctx.enter_context(nc.sbuf_tensor("wo_hi", [P, KT, D], F32R))
        wo_lo = ctx.enter_context(nc.sbuf_tensor("wo_lo", [P, KT, D], F32R))
        phase_attention(nc, qk_hi, qk_lo, dv_dram, vb_dram, w_out, o_hi, o_lo, wo_hi, wo_lo, ident)
        phase_output(nc, x, final_norm, o_hi, o_lo, g_dram, out, wo_hi, wo_lo)


def kernel(**inputs):
    import numpy as np
    import concourse.bacc as bacc
    from concourse.bass_utils import run_bass_kernel_spmd

    w_in = np.asarray(inputs["a_w_in"])[0]
    w_v = w_in[:, 2 * D:3 * D].reshape(KT, P, D // CH, CH).transpose(2, 1, 0, 3)
    w_qkg = np.concatenate([w_in[:, :2 * D], w_in[:, 3 * D:]], axis=1).reshape(KT, P, 3 * KT, P).transpose(2, 1, 0, 3)
    arrays = {
        "in_x": np.ascontiguousarray(np.asarray(inputs["x"])[0, ::-1]),
        "in_a_norm": np.ascontiguousarray(np.asarray(inputs["a_norm"])[0]),
        "in_w_v": np.ascontiguousarray(w_v),
        "in_w_qkg": np.ascontiguousarray(w_qkg),
        "in_w_out": np.ascontiguousarray(np.asarray(inputs["a_w_out"])[0]),
        "in_final_norm": np.ascontiguousarray(np.asarray(inputs["final_norm"])),
    }
    nc = bacc.Bacc("TRN2", target_bir_lowering=False, num_devices=1)
    args = [nc.dram_tensor(name, a.shape, mybir.dt.from_np(a.dtype), kind="ExternalInput").ap() for name, a in arrays.items()]
    out = nc.dram_tensor("out", (S, D), F32, kind="ExternalOutput").ap()
    stick_breaking_layer(nc, *args, out)
    result = run_bass_kernel_spmd(nc, [arrays], core_ids=[0]).results[0]["out"]
    return np.ascontiguousarray(result[::-1])[None]
```

```python
import concourse.bass as bass
from concourse import mybir
from contextlib import ExitStack

F32 = mybir.dt.float32
F32R = mybir.dt.float32r
BF16 = mybir.dt.bfloat16
ALU = mybir.AluOpType
ACT = mybir.ActivationFunctionType

P = 128
S = 2048
D = 1024
H = 16
DH = D // H
KT = D // P
NB = S // P
CH = 512
NC = S // CH
CB = CH // P
GB = 2
GT = GB * P
EPS = 1e-6
Z_SCALE = DH ** -0.5

F32_BYTES = 4
TILE = KT * P * F32_BYTES
HEAD = S * F32_BYTES
TOP = 229344
AT_W_HI = TOP - TILE
AT_W_LO = TOP - 2 * TILE
AT_KL = AT_W_LO - 3 * HEAD // NC
AT_KH = AT_KL - HEAD
AT_Q = AT_KH - HEAD
AT_DV = AT_Q - HEAD
AT_SPARE = AT_DV - HEAD
AT_GATE1 = AT_SPARE - HEAD
AT_LAST_HALF = AT_DV - TILE
AT_WO_RAW = TOP - TILE
AT_LAST_O = AT_WO_RAW - CH * F32_BYTES


def place(nc, name, shape, dt, offset):
    return nc.alloc_sbuf_tensor_at(name, shape, dt, offset=offset)


def as_f32(ap):
    return ap.bitcast(F32)


def pass_waits(eng, passed):
    eng.sem_inc(passed, 1)


def rms_chain(nc, dve, chain, count, mean_sq, root, recip, tmp):
    def link(ins):
        nonlocal count
        ins.then_inc(chain, 1)
        count = count + 1
        dve.wait_ge(chain, count)
    link(nc.vector.reciprocal(recip, root))
    link(nc.vector.tensor_tensor(tmp, recip, recip, ALU.mult))
    link(nc.vector.tensor_tensor(tmp, tmp, mean_sq, ALU.mult))
    link(nc.vector.tensor_scalar(tmp, tmp, -0.5, 1.5, ALU.mult, ALU.add))
    link(nc.vector.tensor_tensor(recip, recip, tmp, ALU.mult))
    return count


CHAIN = 5


def phase_norm_and_v(nc, x, xT, a_norm, w_v, w_qkg, v_dram, hT_hi, hT_lo, ident, raw, xT_row, s_tile, s_vout, s_zout,
                     tile0_hi, tile0_lo):
    with ExitStack() as ctx:
        def sb(name, shape, dt):
            return ctx.enter_context(nc.sbuf_tensor(name, shape, dt))

        def pb(name):
            return ctx.enter_context(nc.psum_tensor(name, [P, CH], F32))

        def sem(name):
            return ctx.enter_context(nc.semaphore(name))

        w_hi = sb("wv_hi", [P, KT, CH], F32R)
        w_lo = sb("wv_lo", [P, KT, CH], F32R)
        xt = place(nc, "xt", [P, 2, D], F32, AT_W_LO)
        norm_col = sb("a_norm_col", [P, KT], F32)
        junk = sb("square_junk", [P, D], BF16)
        stg_hi = [sb(f"stage_hi{p}", [P, KT, P], F32R) for p in range(2)]
        stg_lo = [sb(f"stage_lo{p}", [P, KT, P], F32R) for p in range(2)]
        vst = sb("v_stage", [P, 2, CH], F32)
        stat = sb("stat", [P, 2, 4], F32)
        scale = sb("token_scale", [P, NB], F32)
        zeros = sb("zeros", [DH // 2, D // (DH // 2)], F32)
        vp = [pb(f"v_ps{p}") for p in range(2)]
        sp_row = [pb(f"scale_row_ps{c}") for c in range(NC)]

        s_ident = sem("ident_ready")
        s_norm = sem("norm_col_loaded")
        s_x = [sem(f"x_loaded{p}") for p in range(2)]
        s_xT = [sem(f"xT_loaded{p}") for p in range(2)]
        s_wraw = [sem(f"wv_raw_loaded{n}") for n in range(8)]
        s_wused = sem("wv_quarter_used")
        s_whi = sem("wv_hi_ready")
        s_wlo = sem("wv_lo_ready")
        s_sumsq = sem("sum_squares_ready")
        s_mean = sem("mean_square_ready")
        s_root = sem("root_ready")
        s_chain = sem("rms_chain")
        s_xn = sem("xT_times_norm")
        s_hi = sem("stage_hi_ready")
        s_lo = sem("stage_lo_ready")
        s_keep_hi = sem("hT_hi_kept")
        s_keep_lo = sem("hT_lo_kept")
        s_v = sem("v_ready")
        s_vst = sem("v_evacuated")
        s_tile0 = sem("tile0_hi_ready")
        s_stage = sem("stage_reloaded")
        s_passed = sem("waits_passed_norm")
        s_zero = sem("zero_row")
        s_srow = sem("scale_turned")

        QW = KT // 2
        quarter = [slice(2 * q, 2 * q + 2) for q in range(QW)]
        spot = [raw[:, 0, :], raw[:, 1, :], raw[:, 0, :], xt[:, 1, :], raw[:, 1, :], raw[:, 0, :], xt[:, 0, :], xt[:, 1, :]]
        w_raw = [place_n.rearrange("p (k n) -> p k n", k=2) for place_n in spot]

        with nc.Block() as block:
            @block.sync
            def _(sp):
                def load_w(n):
                    half, q = n // QW, n % QW
                    sp.dma_start(w_raw[n], w_v[half, :, 2 * q:2 * q + 2, :]).then_inc(s_wraw[n], 16)

                def load_x(s, p, first=False):
                    if not first:
                        sp.wait_ge(s_sumsq, s - 1)
                    sp.dma_start(xt[:, p, :], x[bass.ds(s * P, P), :]).then_inc(s_x[p], 16)

                def load_xT(s, p, first=False):
                    if not first:
                        sp.wait_ge(s_lo, s - 1)
                    sp.dma_start(xT_row[:, p, :], xT[s].rearrange("p k t -> p (k t)")).then_inc(s_xT[p], 16)

                load_xT(0, 0, True)
                sp.dma_start(norm_col[:], a_norm).then_inc(s_norm, 16)
                load_w(0)
                load_xT(1, 1, True)
                load_w(1)
                sp.wait_ge(s_wlo, 1)
                load_w(2)
                load_w(3)
                load_x(0, 0, True)
                load_xT(2, 0)
                sp.wait_ge(s_wlo, 4)
                load_x(1, 1, True)
                load_xT(3, 1)
                load_x(2, 0)
                load_x(3, 1)
                with sp.Fori(2, NB // 2) as i:
                    for p in range(2):
                        load_xT(2 * i + p, p)
                        load_x(2 * i + p, p)
                load_w(4)
                load_w(5)
                for n in (6, 7):
                    sp.wait_ge(s_sumsq, NB - 7 + n)
                    load_w(n)
                for p in (1, 0):
                    sp.wait_ge(s_wlo, 6 - p)
                    sp.dma_start(raw[:, p, :], w_qkg[p].rearrange("p k n -> p (k n)")).then_inc(s_tile[p], 16)
                sp.wait_ge(s_zero, 1)
                sp.dma_start(v_dram[S, :].rearrange("(a n) -> a n", a=DH // 2), zeros[:]).then_inc(s_zout, 16)
                sp.wait_ge(s_vst, 2 * NB)
                sp.dma_start(v_dram[(NB - 1) * P:S, CH:D], vst[:, 1, :]).then_inc(s_vout[1], 16)

            @block.gpsimd
            def _(pool):
                nc.gpsimd.memset(ident[:], 0.0).then_inc(s_ident, 1)
                pool.wait_ge(s_ident, 1)
                nc.gpsimd.affine_select(out=ident[:], in_=ident[:], compare_op=ALU.not_equal, fill=1.0, base=0,
                                        pattern=[[-1, P]], channel_multiplier=1).then_inc(s_ident, 1)
                with pool.Fori(0, NB // 2) as i:
                    for p in range(2):
                        pool.wait_ge(s_lo, 2 * i + p + 1)
                        pass_waits(pool, s_passed)
                        nc.gpsimd.tensor_copy(hT_lo[:, :, bass.ts(2 * i + p, P)], as_f32(stg_lo[p][:])).then_inc(s_keep_lo, 1)

            @block.scalar
            def _(act):
                def squares(s, p, first=False):
                    act.wait_ge(s_x[p], 8 * (s - p) + 16)
                    if not first:
                        act.wait_ge(s_sumsq, s)
                    nc.scalar.activation(junk[:], xt[:, p, :], ACT.Square,
                                         accum_out=stat[:, p, 0:1]).then_inc(s_sumsq, 1)
                    act.wait_ge(s_mean, s + 1)
                    nc.scalar.activation(stat[:, p, 2:3], stat[:, p, 1:2], ACT.Sqrt).then_inc(s_root, 1)

                def stage_hi(s, p, first=False):
                    act.wait_ge(s_xn, s + 1)
                    if not first:
                        act.wait_ge(s_v, s - 1)
                        act.wait_ge(s_keep_hi, s - 1)
                    nc.scalar.activation(stg_hi[p][:].rearrange("p k t -> p (k t)"), xT_row[:, p, :],
                                         ACT.Copy).then_inc(s_hi, 1)

                def evacuate(s, p, block_of_s, half, first=False, stores=True):
                    act.wait_ge(s_v, s + 1)
                    if half == 0:
                        act.wait_ge(s_chain, CHAIN * (s + 1))
                    if not first:
                        act.wait_ge(s_vout[p], 8 * (s - p))
                    nc.scalar.activation(vst[:, p, :], vp[p][:], ACT.Copy,
                                         scale=scale[:, bass.ds(block_of_s, 1)]).then_inc(s_vst, 1)
                    if stores:
                        act.wait_ge(s_vst, s + 1)
                        act.dma_start(v_dram[bass.ds(block_of_s * P, P), half * CH:(half + 1) * CH],
                                      vst[:, p, :]).then_inc(s_vout[p], 16)

                def hi_w(n):
                    if QW <= n < 2 * QW - 1:
                        act.wait_ge(s_wused, n - QW + 1)
                    if n == 2 * QW - 1:
                        act.wait_ge(s_v, NB)
                    act.wait_ge(s_wraw[n], 16)
                    nc.scalar.activation(w_hi[:, quarter[n % QW], :], w_raw[n], ACT.Copy).then_inc(s_whi, 1)

                stage_hi(0, 0, True)
                hi_w(0)
                stage_hi(1, 1, True)
                for n in range(1, QW):
                    hi_w(n)
                squares(0, 0, True)
                stage_hi(2, 0)
                evacuate(0, 0, 0, 0, first=True)
                squares(1, 1)
                stage_hi(3, 1)
                evacuate(1, 1, 1, 0, first=True)
                squares(2, 0)
                squares(3, 1)
                with act.Fori(2, NB // 2) as i:
                    for p in range(2):
                        stage_hi(2 * i + p, p)
                        evacuate(2 * i + p - 2, p, 2 * i + p - 2, 0)
                        squares(2 * i + p, p)
                evacuate(NB - 2, 0, NB - 2, 0)
                for n in range(QW, 2 * QW):
                    hi_w(n)
                evacuate(NB - 1, 1, NB - 1, 0)
                with act.Fori(0, NB // 2 - 1) as i:
                    for p in range(2):
                        evacuate(NB + 2 * i + p, p, 2 * i + p, 1)
                act.wait_ge(s_tile[0], 16)
                nc.scalar.activation(tile0_hi[:], raw[:, 0, :].rearrange("p (k n) -> p k n", k=KT),
                                     ACT.Copy).then_inc(s_tile0, 1)
                evacuate(2 * NB - 2, 0, NB - 2, 1)
                evacuate(2 * NB - 1, 1, NB - 1, 1, stores=False)

            @block.vector
            def _(dve):
                def statistics(s, p):
                    dve.wait_ge(s_sumsq, s + 1)
                    nc.vector.tensor_scalar(stat[:, p, 1:2], stat[:, p, 0:1], 1.0 / D, EPS, ALU.mult, ALU.add).then_inc(s_mean, 1)
                    dve.wait_ge(s_root, s + 1)
                    rms_chain(nc, dve, s_chain, CHAIN * s, stat[:, p, 1:2], stat[:, p, 2:3], scale[:, bass.ds(s, 1)], stat[:, p, 3:4])

                def normed(s, p):
                    dve.wait_ge(s_xT[p], 8 * (s - p) + 16)
                    block = xT_row[:, p, :].rearrange("p (k t) -> p k t", k=KT)
                    nc.vector.tensor_tensor(block, block, norm_col[:].unsqueeze(2).to_broadcast([P, KT, P]),
                                            ALU.mult).then_inc(s_xn, 1)

                def stage_lo(s, p, first=False):
                    if not first:
                        dve.wait_ge(s_keep_lo, s - 1)
                    dve.wait_ge(s_hi, s + 1)
                    nc.vector.tensor_tensor(stg_lo[p][:].rearrange("p k t -> p (k t)"), xT_row[:, p, :],
                                            as_f32(stg_hi[p][:]).rearrange("p k t -> p (k t)"), ALU.subtract).then_inc(s_lo, 1)

                def keep_hi(s, p):
                    nc.vector.tensor_copy(hT_hi[:, :, bass.ds(s * P, P)], as_f32(stg_hi[p][:])).then_inc(s_keep_hi, 1)

                def lo_w(n):
                    dve.wait_ge(s_whi, n + 1)
                    nc.vector.tensor_tensor(w_lo[:, quarter[n % QW], :], w_raw[n],
                                            as_f32(w_hi[:, quarter[n % QW], :]), ALU.subtract).then_inc(s_wlo, 1)

                dve.wait_ge(s_norm, 16)
                normed(0, 0)
                stage_lo(0, 0, True)
                lo_w(0)
                normed(1, 1)
                stage_lo(1, 1, True)
                for n in range(1, QW):
                    lo_w(n)
                keep_hi(0, 0)
                keep_hi(1, 1)
                normed(2, 0)
                statistics(0, 0)
                stage_lo(2, 0)
                keep_hi(2, 0)
                normed(3, 1)
                statistics(1, 1)
                stage_lo(3, 1)
                keep_hi(3, 1)
                statistics(2, 0)
                normed(4, 0)
                statistics(3, 1)
                with dve.Fori(2, NB // 2 - 1) as i:
                    for p in range(2):
                        stage_lo(2 * i + p, p)
                        keep_hi(2 * i + p, p)
                        normed(2 * i + p + 1, 1 - p)
                        statistics(2 * i + p, p)
                for s in (NB - 2, NB - 1):
                    stage_lo(s, s % 2)
                    keep_hi(s, s % 2)
                    if s < NB - 1:
                        normed(s + 1, 1)
                    statistics(s, s % 2)

                def reload(s, p, cols):
                    dve.wait_ge(s_v, s - 1)
                    nc.vector.tensor_copy(stg_hi[p][:], as_f32(hT_hi[:, :, cols]))
                    nc.vector.tensor_copy(stg_lo[p][:], as_f32(hT_lo[:, :, cols])).then_inc(s_stage, 1)

                dve.wait_ge(s_keep_hi, NB)
                dve.wait_ge(s_keep_lo, NB)
                reload(NB, 0, slice(0, P))
                for n in range(QW, 2 * QW):
                    lo_w(n)
                reload(NB + 1, 1, slice(P, 2 * P))
                nc.vector.memset(zeros[:], 0.0).then_inc(s_zero, 1)
                reload(NB + 2, 0, slice(2 * P, 3 * P))
                for c in range(NC):
                    dve.wait_ge(s_srow, c + 1)
                    nc.vector.tensor_copy(xT_row[:].rearrange("p a n -> p (a n)")[:, c * CH:(c + 1) * CH], sp_row[c][:])
                reload(NB + 3, 1, slice(3 * P, 4 * P))
                with dve.Fori(2, NB // 2) as i:
                    for p in range(2):
                        reload(NB + 2 * i + p, p, bass.ts(2 * i + p, P))
                dve.wait_ge(s_tile0, 1)
                nc.vector.tensor_tensor(tile0_lo[:], raw[:, 0, :].rearrange("p (k n) -> p k n", k=KT),
                                        as_f32(tile0_hi[:]), ALU.subtract)

            @block.tensor
            def _(pe):
                def products(p, ks):
                    for k in ks:
                        for n, (a, b) in enumerate(((stg_hi, w_hi), (stg_hi, w_lo), (stg_lo, w_hi))):
                            last = nc.tensor.matmul(vp[p][:], a[p][:, k, :], b[:, k, :],
                                                    start=(k == 0 and n == 0), stop=(k == KT - 1 and n == 2))
                    return last

                def project(s, p, staged, count, leaves=False, arrives=False):
                    pe.wait_ge(staged, count)
                    pe.wait_ge(s_vst, s - 1)
                    for q in range(QW):
                        if arrives:
                            pe.wait_ge(s_wlo, QW + q + 1)
                        last = products(p, range(2 * q, 2 * q + 2))
                        if leaves and q < QW - 1:
                            last.then_inc(s_wused, 1)
                    last.then_inc(s_v, 1)

                for q in range(QW):
                    pe.wait_ge(s_wlo, q + 1)
                    for p in range(2):
                        if q == 0:
                            pe.wait_ge(s_lo, p + 1)
                        last = products(p, range(2 * q, 2 * q + 2))
                        if q == QW - 1:
                            last.then_inc(s_v, 1)
                with pe.Fori(1, NB // 2 - 1) as i:
                    for p in range(2):
                        project(2 * i + p, p, s_lo, 2 * i + p + 1)
                project(NB - 2, 0, s_lo, NB - 1)
                project(NB - 1, 1, s_lo, NB, leaves=True)
                project(NB, 0, s_stage, 1, arrives=True)
                project(NB + 1, 1, s_stage, 2)
                pe.wait_ge(s_ident, 2)
                pe.wait_ge(s_chain, CHAIN * NB)
                for b in range(NB):
                    turned = nc.tensor.transpose(sp_row[b // CB][:, (b % CB) * P:(b % CB + 1) * P],
                                                 scale[:, b:b + 1].to_broadcast([P, P]), ident[:])
                    if b % CB == CB - 1:
                        turned.then_inc(s_srow, 1)
                with pe.Fori(1, NB // 2) as i:
                    for p in range(2):
                        project(NB + 2 * i + p, p, s_stage, 2 * i + p + 1)


def phase_qkg(nc, w_qkg, v_dram, qk_hi, qk_lo, g_dram, dv_dram, hT_hi, hT_lo, raw, scale_row, s_wraw, s_vout,
              s_zout, tile0_hi, tile0_lo, head0, s_chunk, dv_head0, s_dv0, s_out, last_half):
    with ExitStack() as ctx:
        def sb(name, shape, dt):
            return ctx.enter_context(nc.sbuf_tensor(name, shape, dt))

        def sem(name):
            return ctx.enter_context(nc.semaphore(name))

        w_raw = raw[:].rearrange("p a (k n) -> p a k n", k=KT)
        w_hi = [tile0_hi, sb("w_hi1", [P, KT, P], F32R)]
        w_lo = [tile0_lo, sb("w_lo1", [P, KT, P], F32R)]
        out_hi = [sb(f"out_hi{h}", [P, NC // 2, CH], F32) for h in range(2)]
        out_lo = [sb("out_lo0", [P, NC // 2, CH], F32), last_half]
        va = place(nc, "v_here", [P, D], F32, AT_Q)
        vb = place(nc, "v_next", [P, D], F32, AT_Q + TILE)
        dv = place(nc, "dv_parts", [P, H, 2, DH], F32R, AT_KH)
        pp = [[ctx.enter_context(nc.psum_tensor(f"proj_ps{p}{c}", [P, CH], F32)) for c in range(NC)] for p in range(2)]

        s_whi1 = sem("tile1_hi_ready")
        s_wlo1 = sem("tile1_lo_ready")
        s_whi = sem("w_hi_ready")
        s_wlo = sem("w_lo_ready")
        s_pp = sem("projection_ready")
        s_scaled = sem("projection_scaled")
        s_ohi = sem("out_hi_ready")
        s_olo = sem("out_lo_ready")
        s_passed = sem("waits_passed_qkg")
        s_va = sem("v_loaded")
        s_dif = sem("dv_ready")
        s_dhi = sem("dv_hi_ready")
        s_dlo = sem("dv_lo_ready")
        s_dout = sem("dv_stored")

        NT = 3 * KT
        NQK = 2 * KT

        with nc.Block() as block:
            @block.sync
            def _(sp):
                sp.dma_start(w_raw[:, 0, :, :], w_qkg[2]).then_inc(s_wraw[0], 16)
                sp.wait_ge(s_zout, 16)
                for p in range(2):
                    sp.wait_ge(s_vout[p], 16 * NB)
                sp.dma_start(va[:], v_dram[0:P, :]).then_inc(s_va, 16)
                sp.dma_start(vb[:], v_dram[1:P + 1, :]).then_inc(s_va, 16)

                def load_dv(t):
                    sp.dma_start(va[:], v_dram[bass.ds(t * P, P), :]).then_inc(s_va, 16)
                    sp.dma_start(vb[:], v_dram[bass.ds(t * P + 1, P), :]).then_inc(s_va, 16)

                def store_dv(t):
                    sp.wait_ge(s_dlo, t + 1)
                    pass_waits(sp, s_passed)
                    sp.dma_start(dv_dram[:, :, t, :].rearrange("h p n -> p h n"),
                                 as_f32(dv[:]).rearrange("p h a n -> p h (a n)")).then_inc(s_dout, 16)

                def load(t, p, first=False):
                    if first:
                        sp.wait_ge(s_wlo1, 1)
                    else:
                        sp.wait_ge(s_wlo, t - 1)
                    sp.dma_start(w_raw[:, p, :, :], w_qkg[t + 2]).then_inc(s_wraw[p], 16)

                def half_ready(t, h):
                    sp.wait_ge(s_olo, NC * t + NC // 2 * (h + 1))
                    return slice(h * S // 2, (h + 1) * S // 2)

                def store(t):
                    rows = bass.ds(t * P, P)
                    for h in range(2):
                        cols = half_ready(t, h)
                        sp.dma_start(qk_hi[rows, cols], out_hi[h][:].rearrange("p c n -> p (c n)")).then_inc(s_out[h], 16)
                        sp.dma_start(qk_lo[rows, cols], out_lo[h][:].rearrange("p c n -> p (c n)")).then_inc(s_out[h], 16)

                def store_gate(t, halves=2):
                    for h in range(halves):
                        cols = half_ready(t, h)
                        sp.dma_start(g_dram[bass.ds((t - NQK) * P, P), cols],
                                     out_lo[h][:].rearrange("p c n -> p (c n)")).then_inc(s_out[h], 16)

                for p in range(2):
                    if p == 1:
                        load(p, p, True)
                    store_dv(p)
                    load_dv(p + 1)
                    store(p)
                with sp.Fori(1, NQK // 2 - 1) as i:
                    for p in range(2):
                        load(2 * i + p, p)
                        store_dv(2 * i + p)
                        load_dv(2 * i + p + 1)
                        store(2 * i + p)
                for p in range(2):
                    load(NQK - 2 + p, p)
                    store_dv(NQK - 2 + p)
                    if p == 0:
                        load_dv(NQK - 1)
                    store(NQK - 2 + p)
                for p in range(2):
                    load(NQK + p, p)
                for h in range(2):
                    sp.wait_ge(s_out[h], 32 * NQK)
                sp.wait_ge(s_dout, 16 * NB)
                for j in range(NC):
                    load_chunk(sp, head0, qk_hi, qk_lo, j, s_chunk[j], with_lo=j < NC - 1)
                sp.dma_start(as_f32(dv_head0[:]), dv_dram[0]).then_inc(s_dv0, 16)
                for p in range(2):
                    store_gate(NQK + p)
                with sp.Fori(NQK // 2 + 1, NT // 2 - 1) as i:
                    for p in range(2):
                        load(2 * i + p, p)
                        store_gate(2 * i + p)
                store_gate(NT - 2)
                store_gate(NT - 1, halves=1)

            @block.gpsimd
            def _(pool):
                def split(t, p):
                    pool.wait_ge(s_wraw[p], 8 * (t - p) + 16)
                    pool.wait_ge(s_pp, NC * (t - 1))
                    pass_waits(pool, s_passed)
                    nc.gpsimd.tensor_copy(w_hi[p][:], w_raw[:, p, :, :]).then_inc(s_whi, 1)
                    pool.wait_ge(s_whi, t - 1)
                    nc.gpsimd.tensor_tensor(w_lo[p][:], w_raw[:, p, :, :], as_f32(w_hi[p][:]), ALU.subtract).then_inc(s_wlo, 1)
                with pool.Fori(1, NT // 2) as i:
                    for p in range(2):
                        split(2 * i + p, p)

            @block.tensor
            def _(pe):
                def tile(t, p, first):
                    if not first:
                        pe.wait_ge(s_wlo, t - 1)
                    elif p == 1:
                        pe.wait_ge(s_wlo1, 1)
                    for c in range(NC):
                        if not first:
                            pe.wait_ge(s_scaled, NC * (t - 2) + c + 1)
                        cols = slice(c * CH, (c + 1) * CH)
                        for k in range(KT):
                            for n, (a, b) in enumerate(((w_hi, hT_hi), (w_hi, hT_lo), (w_lo, hT_hi))):
                                last = nc.tensor.matmul(pp[p][c][:], a[p][:, k, :], b[:, k, cols],
                                                        start=(k == 0 and n == 0), stop=(k == KT - 1 and n == 2))
                        last.then_inc(s_pp, 1)
                for p in range(2):
                    tile(p, p, True)
                with pe.Fori(1, NT // 2) as i:
                    for p in range(2):
                        tile(2 * i + p, p, False)

            @block.scalar
            def _(act):
                def tile_hi(t, func):
                    for c in range(NC):
                        h, n = c // (NC // 2), c % (NC // 2)
                        act.wait_ge(s_scaled, NC * t + c + 1)
                        out = out_hi[h][:, n, :]
                        nc.scalar.activation(out.bitcast(F32R) if func == ACT.Copy else out, out_lo[h][:, n, :],
                                             func).then_inc(s_ohi, 1)

                def dv_hi_of(t, first=False):
                    act.wait_ge(s_dif, t + 1)
                    if not first:
                        act.wait_ge(s_dout, 16 * t)
                    nc.scalar.activation(dv[:, :, 0, :], va[:].rearrange("p (h n) -> p h n", h=H),
                                         ACT.Copy).then_inc(s_dhi, 1)

                act.wait_ge(s_wraw[1], 16)
                nc.scalar.activation(w_hi[1][:], w_raw[:, 1, :, :], ACT.Copy).then_inc(s_whi1, 1)
                for p in range(2):
                    dv_hi_of(p, first=(p == 0))
                    tile_hi(p, ACT.Copy)
                with act.Fori(1, NQK // 2) as i:
                    for p in range(2):
                        dv_hi_of(2 * i + p)
                        tile_hi(2 * i + p, ACT.Copy)
                with act.Fori(NQK // 2, NT // 2) as i:
                    for p in range(2):
                        tile_hi(2 * i + p, ACT.Sigmoid)

            @block.vector
            def _(dve):
                def dv_lo(t):
                    dve.wait_ge(s_dhi, t + 1)
                    nc.vector.tensor_tensor(dv[:, :, 1, :], va[:].rearrange("p (h n) -> p h n", h=H),
                                            as_f32(dv[:, :, 0, :]), ALU.subtract).then_inc(s_dlo, 1)

                def dif(t):
                    dve.wait_ge(s_va, 32 * (t + 1))
                    nc.vector.tensor_tensor(va[:], vb[:], va[:], ALU.subtract).then_inc(s_dif, 1)

                def tile_lo(t, p, op, stores):
                    def second(c):
                        h, n = c // (NC // 2), c % (NC // 2)
                        dve.wait_ge(s_ohi, NC * t + c + 1)
                        nc.vector.tensor_tensor(out_lo[h][:, n, :], out_lo[h][:, n, :], out_hi[h][:, n, :], op).then_inc(s_olo, 1)
                    for c in range(NC):
                        h, n = c // (NC // 2), c % (NC // 2)
                        if stores is not None and n == 0:
                            dve.wait_ge(s_out[h], stores)
                        dve.wait_ge(s_pp, NC * t + c + 1)
                        nc.vector.tensor_tensor(out_lo[h][:, n, :], pp[p][c][:], scale_row[:, c * CH:(c + 1) * CH],
                                                ALU.mult).then_inc(s_scaled, 1)
                        second(c)
                dve.wait_ge(s_whi1, 1)
                nc.vector.tensor_tensor(w_lo[1][:], w_raw[:, 1, :, :], as_f32(w_hi[1][:]), ALU.subtract).then_inc(s_wlo1, 1)
                for p in range(2):
                    dif(p)
                    dv_lo(p)
                    tile_lo(p, p, ALU.subtract, 32 * p if p else None)
                with dve.Fori(1, NQK // 2) as i:
                    for p in range(2):
                        dif(2 * i + p)
                        dv_lo(2 * i + p)
                        tile_lo(2 * i + p, p, ALU.subtract, 64 * i + 32 * p)
                with dve.Fori(NQK // 2, NT // 2) as i:
                    for p in range(2):
                        tile_lo(2 * i + p, p, ALU.mult, 16 * (2 * i + p) + 16 * NQK)


def load_chunk(sp, head, qk_hi, qk_lo, j, loaded, with_hi=True, with_lo=True):
    q_t, kh_t, kl_t = head
    cols = slice(j * CH, (j + 1) * CH)
    for half in range(2):
        rows = slice(half * DH, (half + 1) * DH)
        if with_hi:
            sp.dma_start(as_f32(q_t[rows, cols]), (qk_hi, qk_lo)[half][0:DH, cols]).then_inc(loaded, 16)
            sp.dma_start(as_f32(kh_t[rows, cols]), qk_hi[D:D + DH, cols]).then_inc(loaded, 16)
        if with_lo:
            sp.dma_start(as_f32(kl_t[rows, cols]), qk_lo[D:D + DH, cols]).then_inc(loaded, 16)


def head_steps():
    return [(c, j, r) for c in range(NC) for j in range(c, NC) for r in range(CB)]


STEPS = head_steps()
HS = len(STEPS)
PAIR = 2 * HS
LEAD_SCORES = 10
LEAD_SCAN = 7
LEAD_TURN = 3
RU, RZ, RT, RO = 4, 2, 4, 2


def phase_attention(nc, qk_hi, qk_lo, v_dram, dv_dram, g_dram, w_out, o_hi, o_lo, wo_hi, wo_lo, ident, vT, head0,
                    s_chunk, dv_head0, s_dv, s_gout, s_oout, first_hi, first_lo, gate1, s_gate1, last_half, last_o):
    with ExitStack() as ctx:
        def sb(name, shape, dt):
            return ctx.enter_context(nc.sbuf_tensor(name, shape, dt))

        def pb(name):
            return ctx.enter_context(nc.psum_tensor(name, [P, CH], F32))

        def sem(name):
            return ctx.enter_context(nc.semaphore(name))

        q_t = [head0[0], sb("q_parts1", [P, S], F32R)]
        kh_t = [head0[1], sb("k_hi_twice1", [P, S], F32R)]
        kl_t = [head0[2], sb("k_lo_twice1", [P, S], F32R)]
        dv_t = [dv_head0, sb("dv_head1", [P, NB, P], F32R)]
        v_first = place(nc, "v_first_rows", [NB, D], F32, AT_SPARE)
        og_hi = place(nc, "first_o_hi", [P, KT, GT], F32, AT_KL)
        og_lo = place(nc, "first_o_lo", [P, KT, GT], F32, AT_DV)
        gate = place(nc, "first_gate", [P, KT, GT], F32, AT_SPARE)
        u_t = [[sb(f"u{n}_{r}", [P, CH], F32) for r in range(CB)] for n in range(RU)]
        rt_hi = [sb(f"r_turned_hi{n}", [P, CH], F32R) for n in range(RT)]
        rt_lo = [sb(f"r_turned_lo{n}", [P, CH], F32R) for n in range(RT)]
        o_st = [sb("o_stage0", [P, CH], F32), last_o]
        wo_raw = place(nc, "w_out_raw", [P, D], F32, AT_WO_RAW)
        unbroken = sb("unbroken", [P, CH], F32)
        z_ps = [pb(f"z_ps{n}") for n in range(RZ)]
        t_ps = [pb(f"turn_ps{n}") for n in range(RT)]
        o_ps = [pb(f"o_ps{n}") for n in range(RO)]

        s_qk = [sem(f"qk_loaded{p}") for p in range(2)]
        s_const = sem("constants_ready")
        s_z = sem("scores_ready")
        s_u = sem("u_ready")
        s_r = sem("scan_ready")
        s_t = sem("turned")
        s_hi = sem("r_hi_ready")
        s_lo = sem("r_lo_ready")
        s_o = sem("o_ready")
        s_ost = sem("o_evacuated")
        s_vfirst = sem("v_first_loaded")
        s_vturned = sem("v_first_turned")
        s_vT = sem("v_first_ready")
        s_group = [sem(f"first_group_part_loaded{n}") for n in range(2)]
        s_gated = sem("first_group_steps")
        s_passed = sem("waits_passed_attention")
        s_woraw = sem("w_out_raw_loaded")
        s_wohi = sem("w_out_hi_ready")
        s_wolo = sem("w_out_lo_ready")

        NLOAD = 6 * 16

        def score_cols(m):
            c, j, r = STEPS[m % HS]
            return r * P if j == c else 0

        def sigma_block(m):
            c, j, r = STEPS[m % HS]
            return CB - 1 - r if j == c else r

        def turn_width(m):
            c, j, r = STEPS[m % HS]
            return (sigma_block(m) + 1) * P if j == c else CH

        with nc.Block() as block:
            @block.sync
            def _(sp):
                def load(h, p):
                    rows = bass.ds(h * DH, DH)
                    krows = bass.ds(h * DH + D, DH)
                    for half in range(2):
                        part = slice(half * DH, (half + 1) * DH)
                        sp.dma_start(as_f32(q_t[p][part, :]), (qk_hi, qk_lo)[half][rows, :]).then_inc(s_qk[p], 16)
                        sp.dma_start(as_f32(kh_t[p][part, :]), qk_hi[krows, :]).then_inc(s_qk[p], 16)
                        sp.dma_start(as_f32(kl_t[p][part, :]), qk_lo[krows, :]).then_inc(s_qk[p], 16)

                def load_v(h, p):
                    sp.dma_start(as_f32(dv_t[p][:]), dv_dram[h]).then_inc(s_dv[p], 16)

                sp.dma_start(g_dram[D - P:D, S // 2:S], last_half[:].rearrange("p c n -> p (c n)")).then_inc(s_gout[1], 16)
                load_chunk(sp, head0, qk_hi, qk_lo, NC - 1, s_chunk[NC - 1], with_hi=False)
                for h in range(2):
                    sp.wait_ge(s_gout[h], 32 * 2 * KT + 16 * KT)
                sp.dma_start(v_first[:], v_dram[0:S, :].rearrange("(b p) n -> b p n", p=P)[:, 0, :]).then_inc(s_vfirst, 16)
                load(1, 1)
                load_v(1, 1)
                sp.dma_start(gate1[:], g_dram.rearrange("(k p) t -> p k t", p=P)[:, :, GT:2 * GT]).then_inc(s_gate1, 16)

                def store(pairs, g):
                    c, p = g % NC, g // NC
                    sp.wait_ge(s_ost, NC * 2 * pairs + g + 1)
                    pass_waits(sp, s_passed)
                    rows = bass.ds((2 * pairs + p) * DH, DH)
                    sp.dma_start(o_hi[rows, c * CH:(c + 1) * CH], o_st[c % RO][0:DH, :]).then_inc(s_oout[c % RO], 16)
                    sp.dma_start(o_lo[rows, c * CH:(c + 1) * CH], o_st[c % RO][DH:P, :]).then_inc(s_oout[c % RO], 16)

                with sp.Fori(0, H // 2 - 1) as i:
                    for p in range(2):
                        for c in range(NC):
                            store(i, NC * p + c)
                        load(2 * i + 2 + p, p)
                        load_v(2 * i + 2 + p, p)

                def load_group(part, rows):
                    k = slice(rows.start // P, rows.stop // P)
                    for tile, src in ((gate, g_dram), (og_hi, o_hi), (og_lo, o_lo)):
                        sp.dma_start(tile[:, k, :], src[rows, 0:GT].rearrange("(k p) t -> p k t", p=P)).then_inc(s_group[part], 16)
                for g in range(2 * NC - 1):
                    store(H // 2 - 1, g)
                    if g == NC - 1:
                        for n in range(2):
                            sp.wait_ge(s_oout[n], 32 * (H - 1) * NC // 2)
                        load_group(0, slice(0, (KT - 1) * P))
                    if g == NC:
                        sp.wait_ge(s_oout[0], 32 * ((H - 1) * NC // 2 + 1))
                        load_group(1, slice((KT - 1) * P, D))

            @block.gpsimd
            def _(pool):
                nc.gpsimd.memset(unbroken[:], 1.0).then_inc(s_const, 1)
                pool.wait_ge(s_const, 1)
                nc.gpsimd.affine_select(out=unbroken[:], in_=unbroken[:], compare_op=ALU.is_ge, fill=0.0, base=0,
                                        pattern=[[-1, CH]], channel_multiplier=1).then_inc(s_const, 1)
                for k in range(KT):
                    if k:
                        pool.wait_ge(s_wolo, k)
                    pool.dma_start(wo_raw[:], w_out[k * P:(k + 1) * P, :]).then_inc(s_woraw, 16)
                    pool.wait_ge(s_woraw, 16 * (k + 1))
                    nc.gpsimd.tensor_copy(wo_hi[:, k, :], wo_raw[:]).then_inc(s_wohi, 1)
                    pool.wait_ge(s_wohi, k + 1)
                    nc.gpsimd.tensor_tensor(wo_lo[:, k, :], wo_raw[:], as_f32(wo_hi[:, k, :]), ALU.subtract).then_inc(s_wolo, 1)

                done = 0

                def link(ins):
                    nonlocal done
                    done += 1
                    ins.then_inc(s_gated, 1)
                    pool.wait_ge(s_gated, done)
                pool.wait_ge(s_vT, 1)
                for part, k in enumerate((slice(0, KT - 1), slice(KT - 1, KT))):
                    pool.wait_ge(s_group[part], 48)
                    link(nc.gpsimd.tensor_tensor(og_hi[:, k, :], og_hi[:, k, :], og_lo[:, k, :], ALU.add))
                    blocks = og_hi[:, k, :].rearrange("p k (b t) -> p k b t", t=P)
                    start_v = vT[:, k, 0:GB].unsqueeze(3).to_broadcast([P, k.stop - k.start, GB, P])
                    link(nc.gpsimd.tensor_tensor(blocks, blocks, start_v, ALU.add))
                    link(nc.gpsimd.tensor_tensor(og_hi[:, k, :], og_hi[:, k, :], gate[:, k, :], ALU.mult))
                    link(nc.gpsimd.tensor_copy(first_hi[:, k, :], og_hi[:, k, :]))
                    link(nc.gpsimd.tensor_tensor(first_lo[:, k, :], og_hi[:, k, :], as_f32(first_hi[:, k, :]), ALU.subtract))


            def over_pairs(eng, body):
                body(0, True, False)
                with eng.Fori(1, H // 2 - 1) as i:
                    body(i * PAIR, False, False)
                body((H // 2 - 1) * PAIR, False, True)

            @block.tensor
            def _(pe):
                def scores(at, m):
                    p, (c, j, r) = (m // HS) % 2, STEPS[m % HS]
                    lo = score_cols(m)
                    tau = slice(c * CH + r * P, c * CH + (r + 1) * P)
                    sig = slice(j * CH + lo, (j + 1) * CH)
                    out = z_ps[m % RZ][:, 0:CH - lo]
                    nc.tensor.matmul(out, q_t[p][:, tau], kh_t[p][:, sig], start=True, stop=False)
                    nc.tensor.matmul(out, q_t[p][:, tau], kl_t[p][:, sig], start=False, stop=True).then_inc(s_z, 1)

                def scores_waits(at, m, first):
                    p = (m // HS) % 2
                    if first and m < NC * CB:
                        if m % CB == 0:
                            pe.wait_ge(s_chunk[m // CB], NLOAD)
                    elif m % HS == 0:
                        pe.wait_ge(s_qk[p], NLOAD * (at // PAIR + m // PAIR + p))
                    pe.wait_ge(s_u, at + m - RZ + 1)

                def turn(m):
                    c, j, _ = STEPS[m % HS]
                    r = sigma_block(m)
                    unit = (m // CB) % RU
                    for t in range(turn_width(m) // P):
                        lo = t * P if j == c else 0
                        last = nc.tensor.transpose(t_ps[m % RT][:, t * P:(t + 1) * P],
                                                   u_t[unit][t][:, r * P - lo:(r + 1) * P - lo], ident[:])
                    last.then_inc(s_t, 1)

                def scans_for(m):
                    return m - m % CB + CB

                def weigh(m):
                    p, (c, j, r) = (m // HS) % 2, STEPS[m % HS]
                    w = turn_width(m)
                    out = o_ps[c % RO]
                    begin, end = j == c and r == 0, j == NC - 1 and r == CB - 1
                    weights = dv_t[p][:, j * CB + sigma_block(m), :]
                    nc.tensor.matmul(out[:, 0:w], weights, rt_hi[m % RT][:, 0:w], start=begin, stop=False)
                    last = nc.tensor.matmul(out[:, 0:w], weights, rt_lo[m % RT][:, 0:w], start=False, stop=end)
                    if end:
                        last.then_inc(s_o, 1)

                for m in range(LEAD_SCORES):
                    if m % CB == 0:
                        pe.wait_ge(s_chunk[m // CB], NLOAD)
                    if m >= RZ:
                        pe.wait_ge(s_u, m - RZ + 1)
                    scores(0, m)
                for m in range(LEAD_TURN):
                    pe.wait_ge(s_r, scans_for(m))
                    turn(m)
                pe.wait_ge(s_vfirst, 16)
                for k in range(KT):
                    last = nc.tensor.transpose(o_ps[1][:, k * NB:(k + 1) * NB], v_first[:, k * P:(k + 1) * P], ident[0:NB, 0:NB])
                last.then_inc(s_vturned, 1)

                def pair(at, first, last):
                    for n in range(PAIR):
                        if n % HS == 0:
                            pe.wait_ge(s_dv[n // HS], 16 * (at // PAIR + 1))
                        if n + LEAD_SCORES < PAIR or not last:
                            scores_waits(at, n + LEAD_SCORES, first)
                            scores(at, n + LEAD_SCORES)
                        if n + LEAD_TURN < PAIR or not last:
                            pe.wait_ge(s_r, at + scans_for(n + LEAD_TURN))
                            turn(n + LEAD_TURN)
                        pe.wait_ge(s_lo, at + n + 1)
                        weigh(n)
                over_pairs(pe, pair)

            @block.scalar
            def _(act):
                def stick(at, m):
                    w = CH - score_cols(m)
                    act.wait_ge(s_z, at + m + 1)
                    nc.scalar.activation(u_t[(m // CB) % RU][STEPS[m % HS][2]][:, 0:w], z_ps[m % RZ][:, 0:w],
                                         ACT.Sigmoid, scale=-Z_SCALE).then_inc(s_u, 1)

                def hi(at, m):
                    w = turn_width(m)
                    act.wait_ge(s_t, at + m + 1)
                    nc.scalar.activation(rt_hi[m % RT][:, 0:w], t_ps[m % RT][:, 0:w], ACT.Copy).then_inc(s_hi, 1)

                def chunk_end(m):
                    c, j, r = STEPS[m % HS]
                    return NC * (m // HS) + c if j == NC - 1 and r == CB - 1 else None

                def empty(at, g, first):
                    c, pairs = g % NC, at // PAIR
                    act.wait_ge(s_o, NC * 2 * pairs + g + 1)
                    if not (first and g < RO):
                        act.wait_ge(s_oout[c % RO], 32 * (NC * pairs + g // RO))
                    nc.scalar.activation(o_st[c % RO][:], o_ps[c % RO][:], ACT.Copy).then_inc(s_ost, 1)

                for m in range(LEAD_SCAN):
                    stick(0, m)
                for m in range(LEAD_TURN):
                    stick(0, m + LEAD_SCAN)
                    hi(0, m)
                act.wait_ge(s_vturned, 1)
                nc.scalar.activation(vT[:].rearrange("p k b -> p (k b)"), o_ps[1][:, 0:KT * NB], ACT.Copy).then_inc(s_vT, 1)

                def pair(at, first, last):
                    for m in range(LEAD_TURN, PAIR + LEAD_TURN):
                        if m + LEAD_SCAN < PAIR or not last:
                            stick(at, m + LEAD_SCAN)
                        done = chunk_end(m - LEAD_TURN)
                        if done is not None:
                            empty(at, done, first)
                        if m < PAIR or not last:
                            hi(at, m)
                over_pairs(act, pair)

            @block.vector
            def _(dve):
                def scan(at, m):
                    c, j, r = STEPS[m % HS]
                    u = u_t[(m // CB) % RU][r][:, 0:CH - score_cols(m)]
                    start, other, op = 1.0, unbroken[:, 0:CH - score_cols(m)], ALU.max
                    if j != c:
                        other, op = u, ALU.min
                        w = CH - score_cols(m - CB)
                        start = u_t[(m // CB - 1) % RU][r][:, w - 1:w]
                        dve.wait_ge(s_r, at + m - CB + 1)
                    dve.wait_ge(s_u, at + m + 1)
                    nc.vector.tensor_tensor_scan(u, u, other, start, ALU.mult, op).then_inc(s_r, 1)

                def lo(at, m):
                    w = turn_width(m)
                    dve.wait_ge(s_hi, at + m + 1)
                    nc.vector.tensor_tensor(rt_lo[m % RT][:, 0:w], t_ps[m % RT][:, 0:w],
                                            as_f32(rt_hi[m % RT][:, 0:w]), ALU.subtract).then_inc(s_lo, 1)

                dve.wait_ge(s_const, 2)
                for m in range(LEAD_SCAN):
                    scan(0, m)

                def pair(at, first, last):
                    for m in range(PAIR):
                        if m + LEAD_SCAN < PAIR or not last:
                            scan(at, m + LEAD_SCAN)
                        lo(at, m)
                over_pairs(dve, pair)


def phase_output(nc, x, final_norm, o_hi, o_lo, g_dram, out, wo_hi, wo_lo, vT, s_oout, first_hi, first_lo, gate1,
                 s_gate1, last_o):
    with ExitStack() as ctx:
        def sb(name, shape, dt):
            return ctx.enter_context(nc.sbuf_tensor(name, shape, dt))

        def sem(name):
            return ctx.enter_context(nc.semaphore(name))

        NG = S // GT
        oa = sb("o_part_hi", [P, 2, KT, GT], F32)
        ob = sb("o_part_lo", [P, 2, KT, GT], F32)
        gt = [sb("gate0", [P, KT, GT], F32), gate1]
        norm_row = sb("final_norm_row", [P, D], F32)
        m_hi = [first_hi, sb("gated_hi1", [P, KT, GT], F32R)]
        m_lo = [first_lo, sb("gated_lo1", [P, KT, GT], F32R)]
        xt = sb("x_again", [P, GB, D], F32)
        junk = sb("square_junk2", [P, D], BF16)
        stat = sb("stat2", [P, GB, 5], F32)
        last_sum = sb("last_block_sum", [P, 1], F32)
        yp = [[[ctx.enter_context(nc.psum_tensor(f"y_ps{p}{b}{f}", [P, CH], F32)) for f in range(2)]
               for b in range(GB)] for p in range(2)]

        s_norm = sem("final_norm_loaded")
        s_in = [sem(f"group_loaded{p}") for p in range(2)]
        s_x = [sem(f"x_again_loaded{b}") for b in range(GB)]
        s_sum = sem("o_sums")
        s_gated = sem("gated")
        s_mhi = sem("gated_hi_ready")
        s_mlo = sem("gated_lo_ready")
        s_y = sem("y_ready")
        s_half = sem("last_block_half_ready")
        s_halfres = sem("last_block_half_residual")
        s_res = sem("residual_added")
        s_sumsq = sem("y_sum_squares")
        s_mean = sem("y_mean_square")
        s_root = sem("y_root")
        s_chain = sem("y_rms_chain")
        s_out = sem("out_ready")
        s_stored = [sem(f"out_stored{b}") for b in range(GB)]
        s_last = sem("last_columns_stored")

        def loaded(eng, t, p):
            if p == 1:
                eng.wait_ge(s_in[p], 24 * (t + 1) - 16)
            else:
                eng.wait_ge(s_in[p], 24 * t)

        def sums(eng, ops, t, p):
            ops.tensor_tensor(oa[:, p], oa[:, p], ob[:, p], ALU.add).then_inc(s_sum, 1)
            eng.wait_ge(s_sum, 2 * t - 1)
            blocks = oa[:, p].rearrange("p k (b t) -> p k b t", t=P)
            start_v = vT[:, :, bass.ds(t * GB, GB)].unsqueeze(3).to_broadcast([P, KT, GB, P])
            ops.tensor_tensor(blocks, blocks, start_v, ALU.add).then_inc(s_sum, 1)

        with nc.Block() as block:
            @block.sync
            def _(sp):
                def load(t, p, with_gate=True):
                    sources = [(oa[:, p], o_hi), (ob[:, p], o_lo)] + [(gt[p][:], g_dram)] * with_gate
                    for tile, src in sources:
                        sp.dma_start(tile, src.rearrange("(k p) t -> p k t", p=P)[:, :, bass.ds(t * GT, GT)]).then_inc(s_in[p], 16)

                def load_x(t, b, first):
                    if not first:
                        sp.wait_ge(s_stored[b], 16 * t)
                    sp.dma_start(xt[:, b, :], x[bass.ds(t * GT + b * P, P), :]).then_inc(s_x[b], 16)
                for src, dst in ((last_o[0:DH, :], o_hi), (last_o[DH:P, :], o_lo)):
                    sp.dma_start(dst[D - DH:D, S - CH:S], src).then_inc(s_oout[1], 16)
                load(1, 1, with_gate=False)
                sp.dma_start(norm_row[:], final_norm.rearrange("(a n) -> a n", a=1).to_broadcast([P, D])).then_inc(s_norm, 16)
                for b in range(GB):
                    load_x(0, b, True)
                for n in range(2):
                    sp.wait_ge(s_oout[n], 32 * H * NC // 2)
                load(2, 0)
                for b in range(GB):
                    load_x(1, b, False)

                def ahead(t, p):
                    sp.wait_ge(s_mlo, t - 2)
                    load(t, p)
                    for b in range(GB):
                        load_x(t - 1, b, False)
                with sp.Fori(1, NG // 2 - 1) as i:
                    ahead(2 * i + 1, 1)
                    ahead(2 * i + 2, 0)
                ahead(NG - 1, 1)
                for b in range(GB):
                    load_x(NG - 1, b, False)
                for b in range(GB):
                    sp.wait_ge(s_stored[b], 16 * NG)
                sp.wait_ge(s_last, 16)

            @block.gpsimd
            def _(pool):
                with pool.Fori(1, NG // 2) as i:
                    for p in range(2):
                        loaded(pool, 2 * i + p, p)
                        if p == 0:
                            pool.wait_ge(s_sum, 4 * i - 2)
                        sums(pool, nc.gpsimd, 2 * i + p, p)

            @block.tensor
            def _(pe):
                def group(t, p, first, last_group=False):
                    if not (first and p == 0):
                        pe.wait_ge(s_mlo, t)
                    for b in range(GB):
                        if not first:
                            pe.wait_ge(s_res, GB * (t - 2) + b + 1)
                        tok = slice(b * P, (b + 1) * P)
                        for f in range(2):
                            cols = slice(f * CH, (f + 1) * CH)
                            for k in range(KT):
                                for n, (a, w) in enumerate(((m_hi, wo_hi), (m_hi, wo_lo), (m_lo, wo_hi))):
                                    last = nc.tensor.matmul(yp[p][b][f][:], a[p][:, k, tok], w[:, k, cols],
                                                            start=(k == 0 and n == 0), stop=(k == KT - 1 and n == 2))
                            if last_group and b == GB - 1 and f == 0:
                                last.then_inc(s_half, 1)
                        last.then_inc(s_y, 1)
                for p in range(2):
                    group(p, p, True)
                with pe.Fori(1, NG // 2 - 1) as i:
                    for p in range(2):
                        group(2 * i + p, p, False)
                group(NG - 2, 0, False)
                group(NG - 1, 1, False, last_group=True)

            @block.vector
            def _(dve):
                def gate(t, p, summed_here=False):
                    if summed_here:
                        loaded(dve, t, p)
                        sums(dve, nc.vector, t, p)
                    dve.wait_ge(s_sum, 2 * t)
                    nc.vector.tensor_tensor(oa[:, p], oa[:, p], gt[p][:], ALU.mult).then_inc(s_gated, 1)
                    dve.wait_ge(s_mhi, t)
                    nc.vector.tensor_tensor(m_lo[p][:], oa[:, p], as_f32(m_hi[p][:]), ALU.subtract).then_inc(s_mlo, 1)

                def finish(t, p, b):
                    n = GB * t + b
                    dve.wait_ge(s_y, n + 1)
                    dve.wait_ge(s_x[b], 16 * (t + 1))
                    for f in range(2):
                        cols = slice(f * CH, (f + 1) * CH)
                        last = nc.vector.tensor_tensor(xt[:, b, cols], yp[p][b][f][:], xt[:, b, cols], ALU.add)
                    last.then_inc(s_res, 1)
                    norm_block(n, b)

                def finish_last(p, b):
                    n = GB * NG - 1
                    dve.wait_ge(s_x[b], 16 * NG)
                    dve.wait_ge(s_half, 1)
                    nc.vector.tensor_tensor(xt[:, b, 0:CH], yp[p][b][0][:], xt[:, b, 0:CH], ALU.add).then_inc(s_halfres, 1)
                    dve.wait_ge(s_y, n + 1)
                    nc.vector.tensor_tensor(xt[:, b, CH:D], yp[p][b][1][:], xt[:, b, CH:D], ALU.add).then_inc(s_res, 1)
                    dve.wait_ge(s_sumsq, n + 2)
                    nc.vector.tensor_tensor(stat[:, b, 0:1], stat[:, b, 0:1], last_sum[:], ALU.add).then_inc(s_halfres, 1)
                    dve.wait_ge(s_halfres, 2)
                    norm_block(n, b, halves=True)

                def norm_block(n, b, halves=False):
                    dve.wait_ge(s_sumsq, n + 1)
                    nc.vector.tensor_scalar(stat[:, b, 1:2], stat[:, b, 0:1], 1.0 / D, EPS, ALU.mult, ALU.add).then_inc(s_mean, 1)
                    dve.wait_ge(s_root, n + 1)
                    rms_chain(nc, dve, s_chain, CHAIN * n, stat[:, b, 1:2], stat[:, b, 2:3], stat[:, b, 3:4], stat[:, b, 4:5])
                    for cols in (slice(0, CH), slice(CH, D)) if halves else (slice(0, D),):
                        nc.vector.scalar_tensor_tensor(xt[:, b, cols], xt[:, b, cols], stat[:, b, 3:4], norm_row[:, cols],
                                                       ALU.mult, ALU.mult).then_inc(s_out, 1)

                dve.wait_ge(s_gate1, 16)
                gate(1, 1, summed_here=True)
                dve.wait_ge(s_norm, 16)
                for b in range(GB):
                    finish(0, 0, b)
                with dve.Fori(0, NG // 2 - 1) as i:
                    gate(2 * i + 2, 0)
                    for b in range(GB):
                        finish(2 * i + 1, 1, b)
                    gate(2 * i + 3, 1)
                    for b in range(GB):
                        finish(2 * i + 2, 0, b)
                finish(NG - 1, 1, 0)
                finish_last(1, 1)

            @block.scalar
            def _(act):
                def hi(t, p):
                    act.wait_ge(s_gated, t)
                    nc.scalar.activation(m_hi[p][:], oa[:, p], ACT.Copy).then_inc(s_mhi, 1)

                def finish(t, b, first=False):
                    n = GB * t + b
                    act.wait_ge(s_res, n + 1)
                    if not first:
                        act.wait_ge(s_sumsq, n)
                    nc.scalar.activation(junk[:], xt[:, b, :], ACT.Square, accum_out=stat[:, b, 0:1]).then_inc(s_sumsq, 1)
                    act.wait_ge(s_mean, n + 1)
                    nc.scalar.activation(stat[:, b, 2:3], stat[:, b, 1:2], ACT.Sqrt).then_inc(s_root, 1)
                    act.wait_ge(s_out, n + 1)
                    act.dma_start(out[bass.ds(t * GT + b * P, P), :], xt[:, b, :]).then_inc(s_stored[b], 16)

                hi(1, 1)
                for b in range(GB):
                    finish(0, b, first=(b == 0))
                with act.Fori(0, NG // 2 - 1) as i:
                    act.wait_ge(s_y, 2 * GB * i + GB)
                    hi(2 * i + 2, 0)
                    for b in range(GB):
                        finish(2 * i + 1, b)
                    hi(2 * i + 3, 1)
                    for b in range(GB):
                        finish(2 * i + 2, b)
                finish(NG - 1, 0)
                n, b = GB * NG - 1, GB - 1
                act.wait_ge(s_halfres, 1)
                act.wait_ge(s_sumsq, n)
                nc.scalar.activation(junk[:, 0:CH], xt[:, b, 0:CH], ACT.Square, accum_out=last_sum[:]).then_inc(s_sumsq, 1)
                act.wait_ge(s_res, n + 1)
                nc.scalar.activation(junk[:, CH:D], xt[:, b, CH:D], ACT.Square, accum_out=stat[:, b, 0:1]).then_inc(s_sumsq, 1)
                act.wait_ge(s_mean, n + 1)
                nc.scalar.activation(stat[:, b, 2:3], stat[:, b, 1:2], ACT.Sqrt).then_inc(s_root, 1)
                for f in range(2):
                    cols = slice(f * CH, (f + 1) * CH)
                    act.wait_ge(s_out, n + 1 + f)
                    act.dma_start(out[n * P:(n + 1) * P, cols], xt[:, b, cols]).then_inc(s_stored[b] if f == 0 else s_last, 16)


def stick_breaking_layer(nc, x, xT, a_norm, w_v, w_qkg, w_out, final_norm, out):
    def scratch(name, shape, dt):
        return nc.dram_tensor(name, shape, dt, kind="Internal").ap()

    v_dram = scratch("v_rows", [S + 1, D], F32)
    qk_hi = scratch("qk_hi_cols", [2 * D, S], F32)
    qk_lo = scratch("qk_lo_cols", [2 * D, S], F32)
    g_dram = scratch("gate_cols", [D, S], F32)
    dv_dram = scratch("dv_parts_dram", [H, P, NB, P], F32)
    o_hi = scratch("o_hi_cols", [D, S], F32)
    o_lo = scratch("o_lo_cols", [D, S], F32)

    with ExitStack() as ctx:
        def sem(name):
            return ctx.enter_context(nc.semaphore(name))

        ident = ctx.enter_context(nc.sbuf_tensor("ident", [P, P], F32))
        tile0_hi = place(nc, "w_hi0", [P, KT, P], F32R, AT_W_HI)
        tile0_lo = place(nc, "w_lo0", [P, KT, P], F32R, AT_W_LO)
        head0 = [place(nc, name, [P, S], F32R, offset)
                 for name, offset in (("q_parts0", AT_Q), ("k_hi_twice0", AT_KH), ("k_lo_twice0", AT_KL))]
        dv_head0 = place(nc, "dv_head0", [P, NB, P], F32R, AT_DV)
        first_hi = place(nc, "gated_hi0", [P, KT, GT], F32R, AT_Q)
        first_lo = place(nc, "gated_lo0", [P, KT, GT], F32R, AT_KH)
        gate1 = place(nc, "gate1", [P, KT, GT], F32, AT_GATE1)
        last_half = place(nc, "out_lo1", [P, NC // 2, CH], F32, AT_LAST_HALF)
        last_o = place(nc, "o_stage1", [P, CH], F32, AT_LAST_O)
        s_gate1 = sem("gate1_loaded")
        s_tile = [sem(f"w_tile_loaded{p}") for p in range(2)]
        s_vout = [sem(f"v_stored{p}") for p in range(2)]
        s_zout = sem("zero_row_stored")
        s_chunk = [sem(f"first_chunk_loaded{j}") for j in range(NC)]
        s_dv = [sem(f"dv_loaded{p}") for p in range(2)]
        s_gout = [sem(f"half_tile_stored{h}") for h in range(2)]
        s_oout = [sem(f"o_stored{n}") for n in range(RO)]
        with ExitStack() as projections:
            hT_hi = projections.enter_context(nc.sbuf_tensor("hT_hi", [P, KT, S], F32R))
            hT_lo = projections.enter_context(nc.sbuf_tensor("hT_lo", [P, KT, S], F32R))
            raw = projections.enter_context(nc.sbuf_tensor("w_raw", [P, 2, D], F32))
            xT_row = projections.enter_context(nc.sbuf_tensor("x_T_then_scale_row", [P, 2, D], F32))
            phase_norm_and_v(nc, x, xT, a_norm, w_v, w_qkg, v_dram, hT_hi, hT_lo, ident, raw, xT_row, s_tile, s_vout,
                             s_zout, tile0_hi, tile0_lo)
            phase_qkg(nc, w_qkg, v_dram, qk_hi, qk_lo, g_dram, dv_dram, hT_hi, hT_lo, raw,
                      xT_row[:].rearrange("p a n -> p (a n)"), s_tile, s_vout, s_zout, tile0_hi, tile0_lo, head0, s_chunk,
                      dv_head0, s_dv[0], s_gout, last_half)
        vT = ctx.enter_context(nc.sbuf_tensor("v_first_T", [P, KT, NB], F32))
        wo_hi = ctx.enter_context(nc.sbuf_tensor("wo_hi", [P, KT, D], F32R))
        wo_lo = ctx.enter_context(nc.sbuf_tensor("wo_lo", [P, KT, D], F32R))
        phase_attention(nc, qk_hi, qk_lo, v_dram, dv_dram, g_dram, w_out, o_hi, o_lo, wo_hi, wo_lo, ident, vT, head0,
                        s_chunk, dv_head0, s_dv, s_gout, s_oout, first_hi, first_lo, gate1, s_gate1, last_half, last_o)
        phase_output(nc, x, final_norm, o_hi, o_lo, g_dram, out, wo_hi, wo_lo, vT, s_oout, first_hi, first_lo, gate1, s_gate1,
                     last_o)


def kernel(**inputs):
    import numpy as np
    import concourse.bacc as bacc
    from concourse.bass_utils import run_bass_kernel_spmd

    w_in = np.asarray(inputs["a_w_in"])[0]
    w_v = w_in[:, 2 * D:3 * D].reshape(KT, P, D // CH, CH).transpose(2, 1, 0, 3)
    w_qkg = np.concatenate([w_in[:, :2 * D], w_in[:, 3 * D:]], axis=1).reshape(KT, P, 3 * KT, P).transpose(2, 1, 0, 3)
    x = np.ascontiguousarray(np.asarray(inputs["x"])[0, ::-1])
    arrays = {
        "in_x": x,
        "in_xT": np.ascontiguousarray(x.reshape(NB, P, KT, P).transpose(0, 3, 2, 1)),
        "in_a_norm": np.ascontiguousarray(np.asarray(inputs["a_norm"])[0].reshape(KT, P).T),
        "in_w_v": np.ascontiguousarray(w_v),
        "in_w_qkg": np.ascontiguousarray(w_qkg),
        "in_w_out": np.ascontiguousarray(np.asarray(inputs["a_w_out"])[0]),
        "in_final_norm": np.ascontiguousarray(np.asarray(inputs["final_norm"])),
    }
    nc = bacc.Bacc("TRN2", target_bir_lowering=False, num_devices=1)
    args = [nc.dram_tensor(name, a.shape, mybir.dt.from_np(a.dtype), kind="ExternalInput").ap() for name, a in arrays.items()]
    out = nc.dram_tensor("out", (S, D), F32, kind="ExternalOutput").ap()
    stick_breaking_layer(nc, *args, out)
    result = run_bass_kernel_spmd(nc, [arrays], core_ids=[0]).results[0]["out"]
    return np.ascontiguousarray(result[::-1])[None]
```
